# Optimizing a Trainium2 kernel written in Bass

```python
import math
import jax, jax.numpy as jnp
from jax import lax
import numpy as np

D_MODEL = 1024
BATCH = 1
SEQ = 256
DEPTH = 1

GRID_W = 64
CTX_LEN = 256
N_MIXERS = 2
MIXER_GDN = 0
MIXER_POOL = 1
N_DIRS = 2

GDN_HEADS = 8
GDN_HEAD_DIM = 128
GDN_KEY_DIM = GDN_HEADS * GDN_HEAD_DIM
GDN_VALUE_DIM = GDN_HEADS * GDN_HEAD_DIM
GDN_QKV_DIM = 2 * GDN_KEY_DIM + GDN_VALUE_DIM
GDN_AB_DIM = N_DIRS * 2 * GDN_HEADS
GDN_PROJ_DIM = GDN_QKV_DIM + GDN_VALUE_DIM + GDN_AB_DIM
CONV_W = 5
CHUNK = 64

POOL_WINDOWS = (2, 4, 8, 16)
POOL_GROUPS = len(POOL_WINDOWS)
POOL_GROUP_DIM = D_MODEL // POOL_GROUPS

N_EXPERTS = 16
EC_CAPACITY_FACTOR = 2
D_EXPERT = 2048

N_MOD = 6
RMS_EPS = 1e-6


def rmsnorm(x, g):
    xf = x.astype(jnp.float32)
    y = xf * lax.rsqrt(jnp.mean(xf * xf, axis=-1, keepdims=True) + RMS_EPS)
    return (y * g.astype(jnp.float32)).astype(x.dtype)

def l2norm(x):
    xf = x.astype(jnp.float32)
    return xf * lax.rsqrt(jnp.sum(xf * xf, axis=-1, keepdims=True) + RMS_EPS)

def modulate(xn, shift, scale):
    return xn * (1 + scale) + shift

def short_conv(x, w):
    pad = CONV_W // 2
    return lax.conv_general_dilated(x, w[:, None, :], window_strides=(1,), padding=[(pad, pad)],
                                    dimension_numbers=('NWC', 'WIO', 'NWC'),
                                    feature_group_count=x.shape[-1])

def chunk_gated_delta(q, k, v, g, beta, s0):
    f32 = jnp.float32
    B, H, T, DK = q.shape
    DV = v.shape[-1]
    n = T // CHUNK
    q = q.astype(f32).reshape(B, H, n, CHUNK, DK)
    k = k.astype(f32).reshape(B, H, n, CHUNK, DK)
    v = v.astype(f32).reshape(B, H, n, CHUNK, DV)
    g = g.astype(f32).reshape(B, H, n, CHUNK)
    beta = beta.astype(f32).reshape(B, H, n, CHUNK)
    gcum = jnp.cumsum(g, axis=-1)
    incl = jnp.tril(jnp.ones((CHUNK, CHUNK), dtype=bool))
    strict = jnp.tril(jnp.ones((CHUNK, CHUNK), dtype=bool), -1)
    diff = gcum[..., :, None] - gcum[..., None, :]
    decay = jnp.where(incl, jnp.exp(jnp.where(incl, diff, 0.0)), 0.0)
    k_beta = k * beta[..., None]
    v_beta = v * beta[..., None]
    a_low = jnp.where(strict, jnp.einsum('bhnid,bhnjd->bhnij', k_beta, k) * decay, 0.0)
    lmat = a_low + jnp.eye(CHUNK, dtype=f32)
    rhs = jnp.concatenate([v_beta, k_beta * jnp.exp(gcum)[..., None]], axis=-1)
    sol = lax.linalg.triangular_solve(lmat, rhs, left_side=True, lower=True, unit_diagonal=True)
    u_vals, w_keys = sol[..., :DV], sol[..., DV:]
    att = jnp.einsum('bhnid,bhnjd->bhnij', q, k) * decay
    q_dec = q * jnp.exp(gcum)[..., None]
    k_tail = k * jnp.exp(gcum[..., -1:] - gcum)[..., None]
    g_tail = jnp.exp(gcum[..., -1])
    xs = tuple(jnp.moveaxis(t, 2, 0) for t in (u_vals, w_keys, q_dec, att, k_tail, g_tail))

    def step(S, inp):
        u_n, w_n, qd_n, att_n, kt_n, gt_n = inp
        v_new = u_n - jnp.einsum('bhck,bhkv->bhcv', w_n, S)
        o_n = jnp.einsum('bhck,bhkv->bhcv', qd_n, S) + jnp.einsum('bhij,bhjv->bhiv', att_n, v_new)
        S = S * gt_n[..., None, None] + jnp.einsum('bhck,bhcv->bhkv', kt_n, v_new)
        return S, o_n

    s_fin, o = lax.scan(step, s0.astype(f32), xs)
    o = jnp.moveaxis(o, 0, 2).reshape(B, H, T, DV)
    return o, s_fin

def gdn_project(u, w_in, conv_w, a_log, dt_bias):
    B, T, _ = u.shape
    p = u @ w_in
    qkv = jax.nn.silu(short_conv(p[..., :GDN_QKV_DIM], conv_w))
    z = p[..., GDN_QKV_DIM:GDN_QKV_DIM + GDN_VALUE_DIM]
    ab = p[..., GDN_QKV_DIM + GDN_VALUE_DIM:].astype(jnp.float32).reshape(B, T, N_DIRS, 2, GDN_HEADS)
    q = qkv[..., :GDN_KEY_DIM]
    k = qkv[..., GDN_KEY_DIM:2 * GDN_KEY_DIM]
    v = qkv[..., 2 * GDN_KEY_DIM:]
    heads = lambda t: t.reshape(B, T, GDN_HEADS, GDN_HEAD_DIM).transpose(0, 2, 1, 3)
    q = l2norm(heads(q)) * (GDN_HEAD_DIM ** -0.5)
    k = l2norm(heads(k))
    v = heads(v)
    a = ab[:, :, :, 0, :].transpose(2, 0, 3, 1)
    b = ab[:, :, :, 1, :].transpose(2, 0, 3, 1)
    g = -jnp.exp(a_log.astype(jnp.float32))[:, None, :, None] * jax.nn.softplus(
        a + dt_bias.astype(jnp.float32)[:, None, :, None])
    beta = jax.nn.sigmoid(b)
    return q, k, v, z, g, beta

def gdn_out(o, z, o_gain, w_out):
    B, H, T, DV = o.shape
    o = o.transpose(0, 2, 1, 3)
    zf = z.reshape(B, T, H, DV).astype(jnp.float32)
    o = o * lax.rsqrt(jnp.mean(o * o, axis=-1, keepdims=True) + RMS_EPS) * o_gain.astype(jnp.float32) * jax.nn.silu(zf)
    return o.reshape(B, T, H * DV).astype(z.dtype) @ w_out

def gated_deltanet(u, uc, w_in, conv_w, a_log, dt_bias, o_gain, w_out, with_ctx_out):
    ql, kl, vl, zl, gl, bl = gdn_project(u, w_in, conv_w, a_log, dt_bias)
    qc, kc, vc, zc, gc, bc = gdn_project(uc, w_in, conv_w, a_log, dt_bias)
    B = u.shape[0]
    o_lat = 0.0
    o_ctx = 0.0
    for d in range(N_DIRS):
        flip = (lambda t: jnp.flip(t, axis=2)) if d == 1 else (lambda t: t)
        s0 = jnp.zeros((B, GDN_HEADS, GDN_HEAD_DIM, GDN_HEAD_DIM), jnp.float32)
        oc, s_ctx = chunk_gated_delta(flip(qc), flip(kc), flip(vc), flip(gc[d]), flip(bc[d]), s0)
        ol, _ = chunk_gated_delta(flip(ql), flip(kl), flip(vl), flip(gl[d]), flip(bl[d]), s_ctx)
        o_lat = o_lat + flip(ol)
        if with_ctx_out:
            o_ctx = o_ctx + flip(oc)
    y = gdn_out(o_lat, zl, o_gain, w_out)
    yc = gdn_out(o_ctx, zc, o_gain, w_out) if with_ctx_out else None
    return y, yc

def window_mean(x, w, axis):
    n = x.shape[axis]
    cs = jnp.cumsum(x.astype(jnp.float32), axis=axis)
    pad_width = [(0, 0)] * x.ndim
    pad_width[axis] = (1, 0)
    cs = jnp.pad(cs, pad_width)
    pos = jnp.arange(n)
    lo = jnp.clip(pos - w // 2, 0, n)
    hi = jnp.clip(pos + (w - w // 2), 0, n)
    total = jnp.take(cs, hi, axis=axis) - jnp.take(cs, lo, axis=axis)
    shape = [1] * x.ndim
    shape[axis] = n
    count = (hi - lo).astype(jnp.float32).reshape(shape)
    return (total / count).astype(x.dtype)

def pool_mixer(u, w_grp, scale, on_grid):
    B, T, D = u.shape
    if on_grid:
        rows = T // GRID_W
        xg = u.reshape(B, rows, GRID_W, POOL_GROUPS, POOL_GROUP_DIM)
        axes = (2, 1)
    else:
        xg = u.reshape(B, T, POOL_GROUPS, POOL_GROUP_DIM)
        axes = (1,)
    diffs = []
    for gi, w in enumerate(POOL_WINDOWS):
        xi = xg[..., gi, :]
        m = xi
        for ax in axes:
            m = window_mean(m, w, ax)
        diffs.append(m - xi)
    p = jnp.stack(diffs, axis=-2)
    y = jnp.einsum('...gc,gce->...ge', p, w_grp).reshape(B, T, D)
    return y * scale

def ec_moe(u, w_router, w_gate, w_up, w_down):
    B, T, D = u.shape
    cap = (EC_CAPACITY_FACTOR * T) // N_EXPERTS
    aff = jax.nn.softmax((u @ w_router).astype(jnp.float32), axis=-1)
    gates, idx = lax.top_k(jnp.swapaxes(aff, 1, 2), cap)
    bidx = jnp.arange(B)[:, None, None]
    xs = u[bidx, idx]
    hid = jax.nn.silu(jnp.einsum('becd,edf->becf', xs, w_gate)) * jnp.einsum('becd,edf->becf', xs, w_up)
    ys = jnp.einsum('becf,efd->becd', hid, w_down) * gates[..., None].astype(u.dtype)
    return jnp.zeros_like(u).at[bidx, idx].add(ys)

def first_inputs(seed: int = 0) -> dict:
    key = jax.random.key(seed)
    ks = jax.random.split(key, 24)
    f32 = jnp.float32
    n_gdn = len(range(MIXER_GDN, DEPTH, N_MIXERS))
    n_pool = len(range(MIXER_POOL, DEPTH, N_MIXERS))
    nrm = lambda k, shape, s: jax.random.normal(k, shape, f32) * s
    dt = jnp.exp(jax.random.uniform(ks[10], (n_gdn, N_DIRS, GDN_HEADS), f32,
                                    minval=math.log(1e-3), maxval=math.log(1e-1)))
    return {
        'x': nrm(ks[0], (BATCH, SEQ, D_MODEL), 1.0),
        'c': nrm(ks[1], (BATCH, D_MODEL), 1.0),
        'ctx': nrm(ks[2], (BATCH, CTX_LEN, D_MODEL), 1.0),
        'c_ctx': nrm(ks[3], (D_MODEL,), 1.0),
        'w_mod': nrm(ks[4], (DEPTH, D_MODEL, N_MOD * D_MODEL), 0.3 * D_MODEL ** -0.5),
        'b_mod': nrm(ks[5], (DEPTH, N_MOD * D_MODEL), 0.02),
        'norm_mix_g': 1.0 + nrm(ks[6], (DEPTH, D_MODEL), 0.02),
        'norm_ffn_g': 1.0 + nrm(ks[7], (DEPTH, D_MODEL), 0.02),
        'gdn_w_in': nrm(ks[8], (n_gdn, D_MODEL, GDN_PROJ_DIM), D_MODEL ** -0.5),
        'gdn_conv_w': nrm(ks[9], (n_gdn, CONV_W, GDN_QKV_DIM), CONV_W ** -0.5),
        'gdn_a_log': jnp.log(jax.random.uniform(ks[11], (n_gdn, N_DIRS, GDN_HEADS), f32, minval=1.0, maxval=16.0)),
        'gdn_dt_bias': dt + jnp.log(-jnp.expm1(-dt)),
        'gdn_o_gain': 1.0 + nrm(ks[12], (n_gdn, GDN_HEAD_DIM), 0.02),
        'gdn_w_out': nrm(ks[13], (n_gdn, GDN_VALUE_DIM, D_MODEL), GDN_VALUE_DIM ** -0.5),
        'pool_w': nrm(ks[14], (n_pool, POOL_GROUPS, POOL_GROUP_DIM, POOL_GROUP_DIM), POOL_GROUP_DIM ** -0.5),
        'pool_scale': 1.0 + nrm(ks[15], (n_pool, D_MODEL), 0.05),
        'moe_w_router': nrm(ks[16], (DEPTH, D_MODEL, N_EXPERTS), D_MODEL ** -0.5),
        'moe_w_gate': nrm(ks[17], (DEPTH, N_EXPERTS, D_MODEL, D_EXPERT), D_MODEL ** -0.5),
        'moe_w_up': nrm(ks[18], (DEPTH, N_EXPERTS, D_MODEL, D_EXPERT), D_MODEL ** -0.5),
        'moe_w_down': nrm(ks[19], (DEPTH, N_EXPERTS, D_EXPERT, D_MODEL), D_EXPERT ** -0.5),
        'final_g': 1.0 + nrm(ks[20], (D_MODEL,), 0.02),
    }

def first_block(x, c, ctx, c_ctx, w_mod, b_mod, norm_mix_g, norm_ffn_g,
              gdn_w_in, gdn_conv_w, gdn_a_log, gdn_dt_bias, gdn_o_gain, gdn_w_out,
              pool_w, pool_scale, moe_w_router, moe_w_gate, moe_w_up, moe_w_down, final_g):
    h, hc = x, ctx
    c_act = jax.nn.silu(c)
    cc_act = jax.nn.silu(c_ctx)
    for i in range(DEPTH):
        kind = i % N_MIXERS
        j = i // N_MIXERS
        ctx_carry = any(l % N_MIXERS == MIXER_GDN for l in range(i + 1, DEPTH))
        mod = c_act @ w_mod[i] + b_mod[i]
        sh_m, sc_m, gt_m, sh_f, sc_f, gt_f = [t[:, None, :] for t in jnp.split(mod, N_MOD, axis=-1)]
        u = modulate(rmsnorm(h, norm_mix_g[i]), sh_m, sc_m)
        uc = None
        mod_c = None
        if kind == MIXER_GDN or ctx_carry:
            mod_c = jnp.split(cc_act @ w_mod[i] + b_mod[i], N_MOD, axis=-1)
            uc = modulate(rmsnorm(hc, norm_mix_g[i]), mod_c[0], mod_c[1])
        if kind == MIXER_GDN:
            y, yc = gated_deltanet(u, uc, gdn_w_in[j], gdn_conv_w[j], gdn_a_log[j], gdn_dt_bias[j],
                                   gdn_o_gain[j], gdn_w_out[j], ctx_carry)
        else:
            y = pool_mixer(u, pool_w[j], pool_scale[j], True)
            yc = pool_mixer(uc, pool_w[j], pool_scale[j], False) if ctx_carry else None
        h = h + gt_m * y
        h = h + gt_f * ec_moe(modulate(rmsnorm(h, norm_ffn_g[i]), sh_f, sc_f),
                              moe_w_router[i], moe_w_gate[i], moe_w_up[i], moe_w_down[i])
        if ctx_carry:
            hc = hc + mod_c[2] * yc
            hc = hc + mod_c[5] * ec_moe(modulate(rmsnorm(hc, norm_ffn_g[i]), mod_c[3], mod_c[4]),
                                        moe_w_router[i], moe_w_gate[i], moe_w_up[i], moe_w_down[i])
    return rmsnorm(h, final_g)


DEPTH_2 = 2

Q_BLOCK = 128
D_RNN = 1024
N_RNN_BLOCKS = 8
RNN_BLOCK = D_RNN // N_RNN_BLOCKS
CONV_WIDTH = 4
LRU_C = 8.0
N_HEADS = 16
HEAD_DIM = 64
D_ATTN = N_HEADS * HEAD_DIM
D_FF = 2816
EPS = 1e-6
N_BRANCH = 2
OFF_LRU_X = 0
OFF_LRU_G = OFF_LRU_X + D_RNN
OFF_Q = OFF_LRU_G + D_RNN
OFF_K = OFF_Q + D_ATTN
OFF_V = OFF_K + D_ATTN
OFF_F = OFF_V + D_ATTN
OFF_GATE = OFF_F + N_HEADS
D_IN = OFF_GATE + N_BRANCH * D_MODEL


def rms_norm(x, g):
    xf = x.astype(jnp.float32)
    y = xf * lax.rsqrt(jnp.mean(xf * xf, axis=-1, keepdims=True) + EPS)
    return (y * g.astype(jnp.float32)).astype(x.dtype)

def swiglu_ffn(h, w_up, w_down):
    gate, up = jnp.split(h @ w_up, 2, axis=-1)
    return (jax.nn.silu(gate) * up) @ w_down

def causal_depthwise_conv(x, w, b):
    y = lax.conv_general_dilated(
        x, w[:, None, :].astype(x.dtype), window_strides=(1,),
        padding=[(CONV_WIDTH - 1, 0)],
        dimension_numbers=("NWC", "WIO", "NWC"),
        feature_group_count=x.shape[-1])
    return y + b

def rg_lru(x, w_a, b_a, w_x, b_x, lam):
    bsz, seq, _ = x.shape
    xb = x.reshape(bsz, seq, N_RNN_BLOCKS, RNN_BLOCK)
    r = jax.nn.sigmoid((jnp.einsum("bsnc,ncd->bsnd", xb, w_a).reshape(bsz, seq, D_RNN) + b_a).astype(jnp.float32))
    i = jax.nn.sigmoid((jnp.einsum("bsnc,ncd->bsnd", xb, w_x).reshape(bsz, seq, D_RNN) + b_x).astype(jnp.float32))
    log_a = -LRU_C * r * jax.nn.softplus(-lam.astype(jnp.float32))
    a = jnp.exp(log_a)
    u = jnp.sqrt(-jnp.expm1(2.0 * log_a)) * (i * x.astype(jnp.float32))

    def combine(left, right):
        a_l, b_l = left
        a_r, b_r = right
        return a_l * a_r, a_r * b_l + b_r

    _, h = lax.associative_scan(combine, (a, u), axis=1)
    return h.astype(x.dtype)

def forgetting_attention(q, k, v, f_logit, g_q, g_k):
    bsz, seq = q.shape[0], q.shape[1]
    qn = rms_norm(q, g_q).transpose(0, 2, 1, 3)
    kn = rms_norm(k, g_k).transpose(0, 2, 1, 3)
    vh = v.transpose(0, 2, 1, 3)
    cum = jnp.cumsum(jax.nn.log_sigmoid(f_logit.astype(jnp.float32)), axis=1).transpose(0, 2, 1)
    scale = HEAD_DIM ** -0.5
    outs = []
    for blk in range(seq // Q_BLOCK):
        q0 = blk * Q_BLOCK
        q1 = q0 + Q_BLOCK
        s = jnp.einsum("bhqd,bhkd->bhqk", qn[:, :, q0:q1], kn[:, :, :q1]).astype(jnp.float32) * scale
        s = s + cum[:, :, q0:q1, None] - cum[:, :, None, :q1]
        mask = jnp.arange(q0, q1)[:, None] >= jnp.arange(q1)[None, :]
        s = jnp.where(mask, s, -jnp.inf)
        p = jax.nn.softmax(s, axis=-1)
        outs.append(jnp.einsum("bhqk,bhkd->bhqd", p.astype(vh.dtype), vh[:, :, :q1]))
    o = jnp.concatenate(outs, axis=2)
    return o.transpose(0, 2, 1, 3).reshape(bsz, seq, D_ATTN)

def second_inputs(seed: int = 0) -> dict:
    key = jax.random.key(seed)
    ks = jax.random.split(key, 24)
    L, D, F = DEPTH_2, D_MODEL, D_FF
    nrm = lambda k, shape, fan_in: jax.random.normal(k, shape, jnp.float32) * (fan_in ** -0.5)
    gain = lambda k, shape: 1.0 + 0.02 * jax.random.normal(k, shape, jnp.float32)
    small = lambda k, shape: 0.01 * jax.random.normal(k, shape, jnp.float32)
    u = jax.random.uniform(ks[13], (L, D_RNN), jnp.float32, 0.9, 0.999)
    a0 = u ** (1.0 / LRU_C)
    lam = jnp.log(a0) - jnp.log1p(-a0)
    return {
        "x": jax.random.normal(ks[0], (BATCH, SEQ, D), jnp.float32),
        "g_ffn1": gain(ks[1], (L, D)),
        "w_up1": nrm(ks[2], (L, D, 2 * F), D),
        "w_down1": nrm(ks[3], (L, F, D), F),
        "g_mix": gain(ks[4], (L, D)),
        "w_in": nrm(ks[5], (L, D, D_IN), D),
        "b_gate": small(ks[6], (L, N_BRANCH * D)),
        "conv_w": nrm(ks[7], (L, CONV_WIDTH, D_RNN), CONV_WIDTH),
        "conv_b": small(ks[8], (L, D_RNN)),
        "w_a": nrm(ks[9], (L, N_RNN_BLOCKS, RNN_BLOCK, RNN_BLOCK), RNN_BLOCK),
        "b_a": small(ks[10], (L, D_RNN)),
        "w_x": nrm(ks[11], (L, N_RNN_BLOCKS, RNN_BLOCK, RNN_BLOCK), RNN_BLOCK),
        "b_x": small(ks[12], (L, D_RNN)),
        "lam": lam,
        "g_q": gain(ks[14], (L, HEAD_DIM)),
        "g_k": gain(ks[15], (L, HEAD_DIM)),
        "b_forget": jax.random.uniform(ks[16], (L, N_HEADS), jnp.float32, 1.0, 6.0),
        "w_lru_out": nrm(ks[17], (L, D_RNN, D), D_RNN),
        "w_attn_out": nrm(ks[18], (L, D_ATTN, D), D_ATTN),
        "w_o": nrm(ks[19], (L, D, D), D),
        "g_ffn2": gain(ks[20], (L, D)),
        "w_up2": nrm(ks[21], (L, D, 2 * F), D),
        "w_down2": nrm(ks[22], (L, F, D), F),
    }

def second_block(x, g_ffn1, w_up1, w_down1, g_mix, w_in, b_gate, conv_w, conv_b,
              w_a, b_a, w_x, b_x, lam, g_q, g_k, b_forget, w_lru_out, w_attn_out,
              w_o, g_ffn2, w_up2, w_down2):
    bsz, seq, _ = x.shape
    assert seq % CHUNK == 0 and seq % Q_BLOCK == 0
    for l in range(DEPTH_2):
        x = x + 0.5 * swiglu_ffn(rms_norm(x, g_ffn1[l]), w_up1[l], w_down1[l])

        h = rms_norm(x, g_mix[l])
        z = h @ w_in[l]
        z_lx = z[..., OFF_LRU_X:OFF_LRU_G]
        z_lg = z[..., OFF_LRU_G:OFF_Q]
        q = z[..., OFF_Q:OFF_K].reshape(bsz, seq, N_HEADS, HEAD_DIM)
        k = z[..., OFF_K:OFF_V].reshape(bsz, seq, N_HEADS, HEAD_DIM)
        v = z[..., OFF_V:OFF_F].reshape(bsz, seq, N_HEADS, HEAD_DIM)
        f_logit = z[..., OFF_F:OFF_GATE] + b_forget[l]
        gates = jax.nn.sigmoid(z[..., OFF_GATE:] + b_gate[l])
        gate_lru, gate_attn = jnp.split(gates, N_BRANCH, axis=-1)

        xr = causal_depthwise_conv(z_lx, conv_w[l], conv_b[l])
        hr = rg_lru(xr, w_a[l], b_a[l], w_x[l], b_x[l], lam[l])
        y_lru = (jax.nn.gelu(z_lg) * hr) @ w_lru_out[l]

        o = forgetting_attention(q, k, v, f_logit, g_q[l], g_k[l])
        y_attn = o @ w_attn_out[l]

        m = gate_lru * y_lru + gate_attn * y_attn
        x = x + m @ w_o[l]

        x = x + 0.5 * swiglu_ffn(rms_norm(x, g_ffn2[l]), w_up2[l], w_down2[l])
    return x


def setup_inputs(seed=0):
    out = dict(first_inputs(seed))
    for name, value in second_inputs(seed + 1).items():
        if name != "x":
            out[name + "_2"] = value
    return out


def reference(
    x, c, ctx, c_ctx, w_mod, b_mod, norm_mix_g, norm_ffn_g, gdn_w_in, gdn_conv_w, gdn_a_log,
    gdn_dt_bias, gdn_o_gain, gdn_w_out, pool_w, pool_scale, moe_w_router, moe_w_gate, moe_w_up,
    moe_w_down, final_g, g_ffn1_2, w_up1_2, w_down1_2, g_mix_2, w_in_2, b_gate_2, conv_w_2,
    conv_b_2, w_a_2, b_a_2, w_x_2, b_x_2, lam_2, g_q_2, g_k_2, b_forget_2, w_lru_out_2,
    w_attn_out_2, w_o_2, g_ffn2_2, w_up2_2, w_down2_2,
):
    x = first_block(
        x, c, ctx, c_ctx, w_mod, b_mod, norm_mix_g, norm_ffn_g, gdn_w_in, gdn_conv_w, gdn_a_log,
        gdn_dt_bias, gdn_o_gain, gdn_w_out, pool_w, pool_scale, moe_w_router, moe_w_gate,
        moe_w_up, moe_w_down, final_g,
    )
    return second_block(
        x, g_ffn1_2, w_up1_2, w_down1_2, g_mix_2, w_in_2, b_gate_2, conv_w_2, conv_b_2, w_a_2,
        b_a_2, w_x_2, b_x_2, lam_2, g_q_2, g_k_2, b_forget_2, w_lru_out_2, w_attn_out_2, w_o_2,
        g_ffn2_2, w_up2_2, w_down2_2,
    )


_drawn_inputs = setup_inputs


def setup_inputs(seed=0):
    import zlib

    import numpy as np

    out = dict(_drawn_inputs(seed))
    spreads = {}
    factors = {'ctx': 4.091,
     'c_ctx': 8.0,
     'b_mod': 2.801,
     'norm_mix_g': 8.0,
     'norm_ffn_g': 8.0,
     'gdn_o_gain': 8.0,
     'g_ffn1_2': 4.462,
     'g_mix_2': 4.825,
     'b_gate_2': 8.0,
     'conv_b_2': 2.822,
     'b_a_2': 26.841,
     'b_x_2': 8.0,
     'g_q_2': 8.0,
     'g_k_2': 8.0,
     'g_ffn2_2': 5.088}
    for name, (base, spread) in spreads.items():
        noise = np.random.default_rng([zlib.crc32(name.encode()), seed]).standard_normal(out[name].shape)
        drawn = base * np.exp(spread * noise) if base else spread * noise
        out[name] = __import__('jax').numpy.asarray(drawn.astype(out[name].dtype))
    for name, factor in factors.items():
        out[name] = (out[name] * factor).astype(out[name].dtype)
    return out
```

```python
from contextlib import ExitStack

import concourse.bass as bass
from concourse import mybir

ALU = mybir.AluOpType
ACT = mybir.ActivationFunctionType
F32 = mybir.dt.float32
AX_X = mybir.AxisListType.X

P = 128
D = 1024
KC = D // P
T = 256
NT = T // P
EPS = 1e-6
HEADS = 8
UNITS = 8
LEVELS = (2, 4, 8, 16, 32, 64)
EXPERTS = 16
CAP = 2 * T // EXPERTS
FE = 2048
NR = 6
SLAB = 4096
MOD_SLABS = 12
EARLY_MOD = 4
LAYERS = 2
FF = 2816
FC = FF // P
AH = 16
HD = 64
LRU_C = 8.0

C_ID = 0
C_ONES = 1
C_ONES2 = 1
C_TIE = 3
C_IOTA = 5
C_BD = 6
C_CAUSAL = 7
N_SHARED = 9
C_TRIU, C_TRIL = 9, 10
C_BIG = 11
C_NEG = 13
C_M1 = 15
C_GT = 17
N_CONST = C_GT + 2 * len(LEVELS)


class Signals:

    def __init__(self, nc, ctx, stage, per_turn):
        self.per = per_turn
        self.sem = {n: ctx.enter_context(nc.semaphore(f"{stage}_{n}")) for n in per_turn}
        self.made = {n: 0 for n in per_turn}

    def next(self, name):
        self.made[name] += 1
        return self.sem[name]

    def value(self, turn, name, count):
        return turn * self.per[name] + count

    def close(self):
        bad = {n: (m, self.per[n]) for n, m in self.made.items() if m != self.per[n]}
        assert not bad, bad


def retire(nc, one, two, others):
    with nc.Block() as block:
        @block.sync
        def _(sp):
            for s in [*one.sem.values(), *two.sem.values(), *others]:
                sp.sem_clear(s)


def first_block_mixer(nc, env):
    a = env.inputs
    with ExitStack() as ctx:
        def sb(name, shape):
            return ctx.enter_context(nc.sbuf_tensor(name, shape, F32))

        const = env.const
        ident = const[:, C_ID, :]
        ones = const[:, C_ONES, :]
        ring = env.ring
        ps = env.ps
        hT = env.hT
        modT = env.modT
        vec = env.vec
        masks = sb("mixer_masks", [P, N_CONST - N_SHARED, P])
        vrow = sb("vec_rows", [P, 2, P])
        xrow = sb("x_rows", [P, 4, D])
        stat = sb("norm_stats", [P, 3, 4])
        uT = sb("uT", [P, KC, 2 * T])
        coef = sb("mix_coef", [P, 2, KC])
        cact = sb("c_act", [P, 2, KC])
        wab = sb("w_ab", [P, KC, 32])
        alog = sb("a_log_rows", [P, 16])
        dtb = sb("dt_rows", [P, 16])
        ab = sb("ab", [P, 4, 32])
        gt1 = sb("gate_tmp", [P, 3, 4, 16])
        gates = sb("gates", [P, 4, 16])
        beta = sb("beta", [P, 4, 16])
        NS = 6
        scal = sb("unit_scalars", [P, NS, 2, 4, HEADS])
        hsc = sb("head_scalars", [P, NS, UNITS])
        cw = sb("conv_taps", [P, 3, 5])
        wh = ring[:, NR - 1, :].rearrange("p (k j c) -> p k j c", k=KC, j=4)
        kT = sb("kT", [P, 2 * T])
        vT = sb("vT", [P, 2 * T])
        qT = sb("qT", [P, T])
        kraw, vraw, qraw = kT, vT, qT
        zs = sb("z_silu", [P, T])
        pk = sb("k_projected", [P, 2 * T])
        pv = sb("v_projected", [P, 2 * T])
        pqz = sb("qz_projected", [P, 2 * T])
        sq = sb("squares", [P, 3 * T])
        rn = sb("rnorm", [P, 3 * T])
        bv = sb("beta_v", [P, 2, 4, P])
        ktail = sb("k_tail", [P, 2, 4, P])
        dec = sb("decay", [P, 2, 4, P])
        mrow = dec[:, 0].rearrange("p t c -> p (t c)")
        sqj = dec[:].rearrange("p d t c -> p (d t c)")
        decT = sb("decayT", [P, 2, 2, P])
        att = sb("attT", [P, 2, 2, P])
        erow = sb("exp_rows", [P, 2, 2, P])
        qd = sb("q_decayed", [P, 2, 2, P])
        B = xrow[:, 0, :].rearrange("p (d t c) -> p d t c", d=2, t=4)
        X = xrow[:, 1, :].rearrange("p (d t c) -> p d t c", d=2, t=4)
        Y = xrow[:, 2, :].rearrange("p (d t c) -> p d t c", d=2, t=4)
        GT = xrow[:, 3, :].rearrange("p (d t c) -> p d t c", d=2, t=4)
        S = sb("state", [P, 2, P])
        W = sb("W", [P, 2, P])
        vn = sb("v_new", [P, 2, P])
        og = sb("o_gated", [P, T])
        oT = sb("oT", [P, HEADS, T])
        NV1 = 89

        s_vec = ctx.enter_context(nc.semaphore("small_loaded"))
        s_x = ctx.enter_context(nc.semaphore("x_loaded"))
        s_ab = ctx.enter_context(nc.semaphore("ab_loaded"))
        s_mod = ctx.enter_context(nc.semaphore("w_mod_late_loaded"))
        s_wh = ctx.enter_context(nc.semaphore("w_head_loaded"))
        s_wo = ctx.enter_context(nc.semaphore("w_out_loaded"))
        pre = Signals(nc, ctx, "mix_pre", {
            "vecT_ps": 0, "vecT": 0, "c_act": 0, "mod_row": 0, "mod_ps": 0, "first_head_ps": 0, "first_head": 0, "xsum": 0, "xn": 0, "xT_ps": 0,
            "xT_out": 0, "uT_ps": 0, "uT_out": 0, "ab_ps": 0, "ab": 0, "softp": 0, "gates": 0, "gcum_ps": 0,
            "gcum": 0, "gexp": 0, "pre_dve": 0, "pre_act": 0, "std": 0})
        hs = Signals(nc, ctx, "head", {
            "head_done": 1, "k_ps": 1, "v_ps": 1, "qz_ps": 1, "p_out": 3, "mod_ps": 1, "mod_row": 1, "modT_ps": 1, "modT": 1, "tap0": 3, "conv": 3, "silu": 3, "sqr": 2,
            "sum_ps": 2, "root": 2, "kq_norm": 2, "tok_ps": 2, "tok": 3, "kk_ps": 1, "qk_ps": 1,
            "row_ps": 1, "arg": 4, "decay": 5, "B": 1, "BT_ps": 2, "G_ps": 2 * len(LEVELS),
            "XY_ps": 2 * len(LEVELS), "XY1": 4, "G": 2 * len(LEVELS), "X": 2 * len(LEVELS) - 2,
            "Y": 2 * len(LEVELS), "att": 2, "kS_ps": 6, "W": 8, "vn_ps": 8, "vn": 8, "S_ps": 6, "S": 6,
            "o_ps": 1, "o_sq": 1, "osum_ps": 1, "o_root": 1, "dself": 16, "zsilu": 1})
        s_h1 = ctx.enter_context(nc.semaphore("y_ps"))
        stage = ctx.enter_context(ExitStack())
        block = stage.enter_context(nc.Block())

        @block.sync
        def _(sp):
            rows = [("c", 8), ("c_ctx", 8), ("b_mod", 48), ("norm_mix_g", 8), ("norm_ffn_g", 8), ("final_g", 8),
                    ("gdn_o_gain", 1)]
            at = 0
            for name, n in rows:
                v = a[name]
                v = v if len(v.shape) == 1 else v.rearrange("a b -> (a b)")
                sp.dma_start(vrow[at:at + n, 0, :], v.rearrange("(n p) -> n p", p=P)).then_inc(s_vec, 16)
                at += n
            assert at == NV1
            sp.dma_start(vrow[0:120, 1, :], a["gdn_conv_w"][0].rearrange("w (n p) -> (w n) p", p=P)).then_inc(s_vec, 16)
            sp.dma_start(const[:], a["const"][:, 0:N_SHARED, :]).then_inc(s_vec, 16)
            sp.dma_start(masks[:], a["const"][:, N_SHARED:, :]).then_inc(s_vec, 16)
            for n in range(4):
                src = a["ctx"] if n < 2 else a["x"]
                sp.dma_start(xrow[:, n, :], src[0, (n % 2) * P:(n % 2 + 1) * P, :]).then_inc(s_x, 16)
            w_mod = a["w_mod"][0].rearrange("(k p) n -> p k n", p=P)
            w_in = a["gdn_w_in"][0].rearrange("(k p) n -> p k n", p=P)
            w_out = a["gdn_w_out"][0].rearrange("(k p) n -> p k n", p=P)
            for n in range(EARLY_MOD):
                env.load(sp, n, w_mod[:, :, n * 512:(n + 1) * 512])
            sp.dma_start(wab[:], w_in[:, :, 4096:4128]).then_inc(s_ab, 16)
            sp.dma_start(alog[:], a["gdn_a_log"].rearrange("o d h -> o (d h)").to_broadcast((P, 16))).then_inc(s_ab, 16)
            sp.dma_start(dtb[:], a["gdn_dt_bias"].rearrange("o d h -> o (d h)").to_broadcast((P, 16))).then_inc(s_ab, 16)
            for j in range(4):
                sp.dma_start(wh[:, :, j, :], w_in[:, :, j * D:j * D + P]).then_inc(s_wh, 16)
            sp.dma_start(ring[:, 4, :].rearrange("p (k n) -> p k n", k=KC), w_mod[:, :, EARLY_MOD * 512:(EARLY_MOD + 1) * 512]).then_inc(s_mod, 16)
            sp.wait_ge(env.slab_free, EARLY_MOD)
            sp.dma_start(ring[:, 3, :].rearrange("p (k n) -> p k n", k=KC), w_out[:, :, 512:1024]).then_inc(s_wo, 16)
            env.moe_prefetch(sp, 0, 3)
            sp.wait_ge(pre.sem["first_head_ps"], 3)
            for j in range(4):
                sp.dma_start(wh[:, :, j, :], w_in[:, :, P + j * D:2 * P + j * D]).then_inc(s_wh, 16)
            with sp.Fori(0, HEADS - 2) as h:
                sp.wait_ge(hs.sem["qz_ps"], hs.value(h, "qz_ps", 1))
                for j in range(4):
                    sp.dma_start(wh[:, :, j, :], w_in[:, :, bass.ds(h * P + (2 * P + j * D), P)]).then_inc(s_wh, 16)
                sp.wait_ge(hs.sem["mod_ps"], hs.value(h, "mod_ps", 1))
                sp.dma_start(ring[:, 4, :].rearrange("p (k n) -> p k n", k=KC), w_mod[:, :, bass.ds(h * 512 + (EARLY_MOD + 1) * 512, 512)]).then_inc(s_mod, 16)
            sp.wait_ge(hs.sem["qz_ps"], HEADS - 1)
            for j in range(4):
                sp.dma_start(wh[:, :, j, :], w_out[:, :, j * P:(j + 1) * P]).then_inc(s_wh, 16)
            sp.wait_ge(hs.sem["mod_ps"], HEADS - 1)
            sp.dma_start(ring[:, 4, :].rearrange("p (k n) -> p k n", k=KC), w_mod[:, :, (MOD_SLABS - 1) * 512:MOD_SLABS * 512]).then_inc(s_mod, 16)
            sp.wait_ge(s_h1, KC)
            env.moe_prefetch(sp, 3, NR)

        @block.tensor
        def _(pe):
            pe.wait_ge(s_vec, 16 * 10)
            nc.tensor.transpose(ps[0][:, 0:NV1], vrow[0:NV1, 0, :], const[0:NV1, C_ID, 0:NV1])
            nc.tensor.transpose(ps[0][:, 128:248], vrow[0:120, 1, :], const[0:120, C_ID, 0:120]).then_inc(pre.next("vecT_ps"), 1)
            pe.wait_ge(s_x, 16 * 4)
            for k in range(KC):
                for t in range(2):
                    i = nc.tensor.transpose(ps[1 + k // 2][:, (k % 2) * T + t * P:(k % 2) * T + t * P + P], xrow[:, 2 + t, k * P:(k + 1) * P], ident)
                if k % 2:
                    i.then_inc(pre.next("xT_ps"), 1)
            pe.wait_ge(pre.sem["c_act"], 1)
            for n in range(EARLY_MOD):
                pe.wait_ge(env.full[n], 16)
                for k in range(KC):
                    i = nc.tensor.matmul(ps[(5, 6, 7, 0)[n]][0:2, :], cact[:, :, k], ring[:, n, k * 512:(k + 1) * 512], start=(k == 0), stop=(k == KC - 1))
                i.then_inc(env.slab_free, 1)
            for n in range(EARLY_MOD):
                pe.wait_ge(pre.sem["mod_row"], n + 1)
            for n in range(EARLY_MOD):
                for j in range(4):
                    i = nc.tensor.matmul(ps[5][:, (n * 4 + j) * 2:(n * 4 + j) * 2 + 2], (bv, ktail)[n // 2][0:2, n % 2, j, :], ident[0:2, 0:2],
                                         start=(n == 0 and j == 0), stop=True, skip_group_check=True)
            i.then_inc(pre.next("mod_ps"), 1)
            pe.wait_ge(pre.sem["xn"], 4)
            pe.wait_ge(pre.sem["xT_out"], 4)
            for k in range(KC):
                if k >= 4:
                    pe.wait_ge(pre.sem["uT_out"], 2 * (k - 3))
                for t in range(4):
                    i = nc.tensor.transpose(ps[1 + k % 4][:, t * P:(t + 1) * P], xrow[:, t, k * P:(k + 1) * P], ident)
                i.then_inc(pre.next("uT_ps"), 1)
            pe.wait_ge(pre.sem["uT_out"], 2 * KC)
            pe.wait_ge(s_ab, 16 * 3)
            for t in range(4):
                for k in range(KC):
                    i = nc.tensor.matmul(ps[6][:, t * 32:t * 32 + 32], uT[:, k, t * P:(t + 1) * P], wab[:, k, :],
                                         start=(t == 0 and k == 0), stop=(k == KC - 1), skip_group_check=True)
            i.then_inc(pre.next("ab_ps"), 1)
            pe.wait_ge(pre.sem["gates"], 1)
            nc.tensor.matmul(ps[7][:, 0:32], masks[:, C_TRIU - N_SHARED, :], gates[:, :, 0:8], start=True, stop=True)
            nc.tensor.matmul(ps[7][:, 32:64], masks[:, C_TRIL - N_SHARED, :], gates[:, :, 8:16], start=False, stop=True, skip_group_check=True)
            nc.tensor.matmul(ps[7][:, 64:96], ones, gates[:, :, 0:8], start=False, stop=True, skip_group_check=True)
            nc.tensor.matmul(ps[7][:, 96:128], ones, gates[:, :, 8:16], start=False, stop=True, skip_group_check=True).then_inc(pre.next("gcum_ps"), 1)

            def project(out, j, tok0, start=True):
                for k in range(KC):
                    i = nc.tensor.matmul(out, wh[:, k, j, :], uT[:, k, tok0:2 * T], start=(start and k == 0), stop=(k == KC - 1),
                                         skip_group_check=True)
                return i

            pe.wait_ge(s_wh, 64)
            project(ps[1][:, :], 1, 0).then_inc(pre.next("first_head_ps"), 1)
            project(ps[2][:, :], 2, 0).then_inc(pre.next("first_head_ps"), 1)
            project(ps[3][:, 0:T], 0, T)
            project(ps[3][:, T:], 3, T, start=False).then_inc(pre.next("first_head_ps"), 1)

            with pe.Fori(0, HEADS) as h:
                pe.wait_ge(hs.sem["head_done"], hs.value(h, "head_done", 1))
                pe.wait_ge(hs.sem["dself"], hs.value(h, "dself", 1))
                for u in range(UNITS):
                    i = nc.tensor.transpose(ps[6 + u // 4][:, (u % 4) * P:(u % 4 + 1) * P], hsc[:, 0, u:u + 1].to_broadcast((P, P)), ident)
                i.then_inc(hs.next("row_ps"), 1)
                pe.wait_ge(s_wh, h * 64 + 128)
                project(ps[1][:, :], 1, 0).then_inc(hs.next("k_ps"), 1)
                pe.wait_ge(hs.sem["sqr"], hs.value(h, "sqr", 1))
                nc.tensor.matmul(ps[3][:, :], ones, sq[:, 0:2 * T], start=True, stop=True).then_inc(hs.next("sum_ps"), 1)
                pe.wait_ge(hs.sem["sqr"], hs.value(h, "sqr", 2))
                nc.tensor.matmul(ps[4][:, 0:T], ones, sq[:, 2 * T:], start=True, stop=True).then_inc(hs.next("sum_ps"), 1)
                project(ps[2][:, :], 2, 0).then_inc(hs.next("v_ps"), 1)
                pe.wait_ge(hs.sem["silu"], hs.value(h, "silu", 2))
                for t in range(4):
                    i = nc.tensor.transpose(ps[5][:, t * P:(t + 1) * P], vT[:, t * P:(t + 1) * P], ident)
                i.then_inc(hs.next("tok_ps"), 1)
                pe.wait_ge(hs.sem["kq_norm"], hs.value(h, "kq_norm", 1))
                pe.wait_ge(hs.sem["silu"], hs.value(h, "silu", 3))
                for t in range(4):
                    i = nc.tensor.matmul(ps[0][:, t * P:(t + 1) * P], kT[:, t * P:(t + 1) * P], kT[:, t * P:(t + 1) * P],
                                         start=(t == 0), stop=True, skip_group_check=True)
                i.then_inc(hs.next("kk_ps"), 1)
                pe.wait_ge(hs.sem["root"], hs.value(h, "root", 1))
                project(ps[3][:, 0:T], 0, T)
                project(ps[3][:, T:], 3, T, start=False).then_inc(hs.next("qz_ps"), 1)
                pe.wait_ge(hs.sem["p_out"], hs.value(h, "p_out", 1))
                for t in range(4):
                    i = nc.tensor.transpose(ps[1][:, t * P:(t + 1) * P], kT[:, t * P:(t + 1) * P], ident)
                i.then_inc(hs.next("tok_ps"), 1)
                pe.wait_ge(hs.sem["kq_norm"], hs.value(h, "kq_norm", 2))
                pe.wait_ge(hs.sem["p_out"], hs.value(h, "p_out", 2))
                for t in range(2):
                    i = nc.tensor.matmul(ps[2][:, t * P:(t + 1) * P], kT[:, T + t * P:T + (t + 1) * P], qT[:, t * P:(t + 1) * P],
                                         start=(t == 0), stop=True, skip_group_check=True)
                i.then_inc(hs.next("qk_ps"), 1)
                pe.wait_ge(hs.sem["B"], hs.value(h, "B", 1))
                pe.wait_ge(hs.sem["tok"], hs.value(h, "tok", 3))
                for d in range(2):
                    for t in range(4):
                        i = nc.tensor.transpose(ps[4 + d][:, t * P:(t + 1) * P], B[:, d, t, :], ident)
                    i.then_inc(hs.next("BT_ps"), 1)
                pe.wait_ge(hs.sem["decay"], hs.value(h, "decay", 5))
                for l in range(len(LEVELS)):
                    for d in range(2):
                        pe.wait_ge(hs.sem["XY1"], hs.value(h, "XY1", 4)) if l == 0 else pe.wait_ge(hs.sem["Y"], hs.value(h, "Y", 2 * (l - 1) + d + 1))
                        for t in range(4):
                            i = nc.tensor.matmul(ps[6 + d][:, t * P:(t + 1) * P], B[:, d, t, :], Y[:, d, t, :],
                                                 start=(t == 0), stop=True, skip_group_check=True)
                        i.then_inc(hs.next("G_ps"), 1)
                    for d in range(2):
                        pe.wait_ge(hs.sem["G"], hs.value(h, "G", 2 * l + d + 1))
                        if l > 0:
                            pe.wait_ge(hs.sem["X"], hs.value(h, "X", 2 * (l - 1) + d + 1))
                        if l == 0:
                            pe.wait_ge(hs.sem["p_out"], hs.value(h, "p_out", 3))
                            pe.wait_ge(hs.sem["B"], hs.value(h, "B", 1))
                            pe.wait_ge(hs.sem["att"], hs.value(h, "att", 2))
                        for t in range(4):
                            if l < len(LEVELS) - 1:
                                nc.tensor.matmul(ps[2 * d][:, t * P:(t + 1) * P], GT[:, d, t, :], X[:, d, t, :],
                                                 start=(t == 0), stop=True, skip_group_check=True)
                            i = nc.tensor.matmul(ps[2 * d + 1][:, t * P:(t + 1) * P], X[:, d, t, :], GT[:, d, t, :],
                                                 start=(t == 0), stop=True, skip_group_check=True)
                        i.then_inc(hs.next("XY_ps"), 1)
                pe.wait_ge(hs.sem["Y"], hs.value(h, "Y", 2 * len(LEVELS)))
                for c in range(4):
                    for d in range(2):
                        t = c if d == 0 else (1, 0, 3, 2)[c]
                        if c > 0:
                            pe.wait_ge(hs.sem["S"], hs.value(h, "S", 2 * (c - 1) + d + 1))
                            nc.tensor.matmul(ps[4 + d][:, 0:P], kT[:, t * P:(t + 1) * P], S[:, d, :], start=True, stop=True).then_inc(hs.next("kS_ps"), 1)
                            if c >= 2:
                                nc.tensor.matmul(ps[0][:, (t - 2) * P:(t - 1) * P], S[:, d, :], qd[:, d, t - 2, :],
                                                 start=(c == 2 and d == 0), stop=False, skip_group_check=True)
                    for d in range(2):
                        t = c if d == 0 else (1, 0, 3, 2)[c]
                        pe.wait_ge(hs.sem["W"], hs.value(h, "W", 2 * c + d + 1))
                        nc.tensor.matmul(ps[6 + d][:, 0:P], Y[:, d, t, :], W[:, d, :], start=True, stop=True).then_inc(hs.next("vn_ps"), 1)
                    if c == 0:
                        pe.wait_ge(s_mod, h * 16 + 16)
                    for k in (2 * c, 2 * c + 1):
                        mm = nc.tensor.matmul(ps[1][0:2, :], cact[:, :, k], ring[:, 4, k * 512:(k + 1) * 512], start=(k == 0), stop=(k == KC - 1))
                    if c == 3:
                        mm.then_inc(hs.next("mod_ps"), 1)
                    for d in range(2):
                        t = c if d == 0 else (1, 0, 3, 2)[c]
                        pe.wait_ge(hs.sem["vn"], hs.value(h, "vn", 2 * c + d + 1))
                        if c < 3:
                            nc.tensor.matmul(ps[2 + d][:, 0:P], ktail[:, d, t, :], vn[:, d, :], start=True, stop=True).then_inc(hs.next("S_ps"), 1)
                        if c >= 2:
                            i = nc.tensor.matmul(ps[0][:, (t - 2) * P:(t - 1) * P], vn[:, d, :], att[:, d, t - 2, :],
                                                 start=False, stop=True, skip_group_check=True)
                i.then_inc(hs.next("o_ps"), 1)
                pe.wait_ge(hs.sem["o_sq"], hs.value(h, "o_sq", 1))
                nc.tensor.matmul(ps[4][:, 0:T], ones, sq[:, 0:T], start=True, stop=True).then_inc(hs.next("osum_ps"), 1)
                pe.wait_ge(hs.sem["mod_row"], hs.value(h, "mod_row", 1))
                for j in range(4):
                    mm = nc.tensor.matmul(ps[5][:, 2 * j:2 * j + 2], mrow[0:2, j * P:(j + 1) * P], ident[0:2, 0:2], start=(j == 0), stop=True,
                                          skip_group_check=True)
                mm.then_inc(hs.next("modT_ps"), 1)

            pe.wait_ge(hs.sem["head_done"], hs.value(HEADS, "head_done", 1))
            pe.wait_ge(s_wo, 16)
            pe.wait_ge(s_wh, 64 * (HEADS + 1))
            for m in range(KC):
                w = ring[:, NR - 1 if m < 4 else 3, :].rearrange("p (k n) -> p k n", k=KC)
                for k in range(KC):
                    i = nc.tensor.matmul(ps[m // 2][:, (m % 2) * T:(m % 2 + 1) * T], w[:, k, (m % 4) * P:(m % 4 + 1) * P], oT[:, k, :],
                                         start=(k == 0 and m % 2 == 0), stop=(k == KC - 1), skip_group_check=True)
                i.then_inc(s_h1, 1)

        @block.scalar
        def _(act):
            act.wait_ge(pre.sem["vecT"], 1)
            nc.scalar.activation(cact[:].rearrange("p c k -> p (c k)"), vec[:, 0:16], ACT.Silu).then_inc(pre.next("c_act"), 1)
            act.wait_ge(s_x, 16 * 4)
            for t in range(4):
                nc.scalar.activation(sqj, xrow[:, t, :], ACT.Square, accum_out=stat[:, 0, t:t + 1]).then_inc(pre.next("xsum"), 1)
                act.wait_ge(pre.sem["xsum"], pre.made["xsum"])
            act.wait_ge(pre.sem["pre_dve"], 1)
            nc.scalar.activation(stat[:, 1, :], stat[:, 2, :], ACT.Sqrt).then_inc(pre.next("std"), 1)
            act.wait_ge(pre.sem["ab"], 1)
            nc.scalar.activation(gt1[:, 1], gt1[:, 0], ACT.Abs).then_inc(pre.next("pre_act"), 1)
            act.wait_ge(pre.sem["pre_act"], 1)
            nc.scalar.activation(gt1[:, 1], gt1[:, 1], ACT.Exp, scale=-1.0).then_inc(pre.next("pre_act"), 1)
            act.wait_ge(pre.sem["pre_act"], 2)
            nc.scalar.activation(alog[:], alog[:], ACT.Exp)
            nc.scalar.activation(gt1[:, 1], gt1[:, 1], ACT.Ln, bias=1.0).then_inc(pre.next("softp"), 1)
            for d in range(2):
                i = nc.scalar.activation(beta[:, :, d * 8:d * 8 + 8], ab[:, :, d * 16 + 8:d * 16 + 16], ACT.Sigmoid)
            i.then_inc(pre.next("softp"), 1)
            act.wait_ge(pre.sem["gcum"], 1)
            nc.scalar.activation(scal[:, 3], scal[:, 3], ACT.Exp)
            nc.scalar.activation(scal[:, 4], scal[:, 4], ACT.Exp)
            nc.scalar.activation(scal[:, 5], scal[:, 0], ACT.Exp).then_inc(pre.next("gexp"), 1)

            for n, dst in enumerate((pk, pv, pqz)):
                act.wait_ge(pre.sem["first_head_ps"], n + 1)
                nc.scalar.activation(dst[:], ps[1 + n][:, :], ACT.Copy).then_inc(pre.next("first_head"), 1)
            with act.Fori(0, HEADS) as h:
                act.wait_ge(hs.sem["head_done"], hs.value(h, "head_done", 1))
                act.wait_ge(hs.sem["dself"], hs.value(h, "dself", 2))
                for n, (raw, src) in enumerate(((kraw, pk[:]), (vraw, pv[:]), (qraw, pqz[:, 0:T]))):
                    nc.scalar.activation(raw[:, :], src, ACT.Copy, scale=cw[:, (1, 2, 0)[n], 2:3]).then_inc(hs.next("tap0"), 1)
                nc.scalar.activation(zs[:, :], pqz[:, T:], ACT.Silu).then_inc(hs.next("zsilu"), 1)
                act.wait_ge(hs.sem["conv"], hs.value(h, "conv", 1))
                nc.scalar.activation(kraw[:, :], kraw[:, :], ACT.Silu).then_inc(hs.next("silu"), 1)
                act.wait_ge(hs.sem["silu"], hs.value(h, "silu", 1))
                nc.scalar.activation(sq[:, 0:2 * T], kraw[:, :], ACT.Square).then_inc(hs.next("sqr"), 1)
                act.wait_ge(hs.sem["conv"], hs.value(h, "conv", 2))
                nc.scalar.activation(vT[:, :], vraw[:, :], ACT.Silu).then_inc(hs.next("silu"), 1)
                act.wait_ge(hs.sem["conv"], hs.value(h, "conv", 3))
                nc.scalar.activation(qraw[:, :], qraw[:, :], ACT.Silu).then_inc(hs.next("silu"), 1)
                act.wait_ge(hs.sem["silu"], hs.value(h, "silu", 3))
                nc.scalar.activation(sq[:, 2 * T:], qraw[:, :], ACT.Square).then_inc(hs.next("sqr"), 1)
                act.wait_ge(hs.sem["sum_ps"], hs.value(h, "sum_ps", 1))
                nc.scalar.activation(rn[:, 0:2 * T], ps[3][:, :], ACT.Sqrt, bias=env.eps[:, 0:1]).then_inc(hs.next("root"), 1)
                act.wait_ge(hs.sem["sum_ps"], hs.value(h, "sum_ps", 2))
                nc.scalar.activation(rn[:, 2 * T:], ps[4][:, 0:T], ACT.Sqrt, bias=env.eps[:, 0:1]).then_inc(hs.next("root"), 1)
                act.wait_ge(hs.sem["k_ps"], hs.value(h, "k_ps", 1))
                nc.scalar.activation(pk[:], ps[1][:, :], ACT.Copy).then_inc(hs.next("p_out"), 1)
                act.wait_ge(hs.sem["v_ps"], hs.value(h, "v_ps", 1))
                nc.scalar.activation(pv[:], ps[2][:, :], ACT.Copy).then_inc(hs.next("p_out"), 1)
                for d in range(2):
                    act.wait_ge(hs.sem["arg"], hs.value(h, "arg", 1 + d))
                    nc.scalar.activation(dec[:, d], dec[:, d], ACT.Exp, scale=-1.0).then_inc(hs.next("decay"), 1)
                for d in range(2):
                    act.wait_ge(hs.sem["arg"], hs.value(h, "arg", 3 + d))
                    nc.scalar.activation(decT[:, d], decT[:, d], ACT.Exp).then_inc(hs.next("decay"), 1)
                for d in range(2):
                    i = nc.scalar.activation(erow[:, d], ps[6 + d][:, 2 * P:].rearrange("p (t c) -> p t c", t=2), ACT.Exp)
                i.then_inc(hs.next("decay"), 1)
                act.wait_ge(hs.sem["qz_ps"], hs.value(h, "qz_ps", 1))
                nc.scalar.activation(pqz[:], ps[3][:, :], ACT.Copy).then_inc(hs.next("p_out"), 1)
                for l in range(len(LEVELS)):
                    for d in range(2):
                        act.wait_ge(hs.sem["XY_ps"], hs.value(h, "XY_ps", 2 * l + d + 1))
                        if l < len(LEVELS) - 1:
                            nc.scalar.activation(X[:, d], ps[2 * d][:, :].rearrange("p (t c) -> p t c", t=4), ACT.Copy).then_inc(hs.next("X"), 1)
                        nc.scalar.activation(Y[:, d], ps[2 * d + 1][:, :].rearrange("p (t c) -> p t c", t=4), ACT.Copy).then_inc(hs.next("Y"), 1)
                for c in range(4):
                    for d in range(2):
                        act.wait_ge(hs.sem["vn_ps"], hs.value(h, "vn_ps", 2 * c + d + 1))
                        nc.scalar.activation(vn[:, d, :], ps[6 + d][:, 0:P], ACT.Copy).then_inc(hs.next("vn"), 1)
                act.wait_ge(hs.sem["o_ps"], hs.value(h, "o_ps", 1))
                nc.scalar.activation(sq[:, 0:T], ps[0][:, 0:T], ACT.Square).then_inc(hs.next("o_sq"), 1)
                act.wait_ge(hs.sem["mod_ps"], hs.value(h, "mod_ps", 1))
                nc.scalar.activation(mrow[0:2, :], ps[1][0:2, :], ACT.Copy).then_inc(hs.next("mod_row"), 1)
                act.wait_ge(hs.sem["osum_ps"], hs.value(h, "osum_ps", 1))
                nc.scalar.activation(rn[:, 0:T], ps[4][:, 0:T], ACT.Sqrt, bias=env.eps[:, 0:1], scale=1.0 / P).then_inc(hs.next("o_root"), 1)

        @block.vector
        def _(dve):
            nc.vector.memset(env.eps[:, 0:1], EPS)
            dve.wait_ge(pre.sem["vecT_ps"], 1)
            nc.vector.tensor_copy(vec[:, 0:NV1], ps[0][:, 0:NV1])
            nc.vector.tensor_copy(vec[:, 96:216], ps[0][:, 128:248]).then_inc(pre.next("vecT"), 1)
            for n in range(4):
                dve.wait_ge(pre.sem["xT_ps"], n + 1)
                nc.vector.tensor_copy(hT[:, 2 * n:2 * n + 2, :], ps[1 + n][:, :].rearrange("p (k t) -> p k t", k=2)).then_inc(pre.next("xT_out"), 1)
            dve.wait_ge(pre.sem["xsum"], 4)
            nc.vector.tensor_scalar(stat[:, 2, :], stat[:, 0, :], 1.0 / D, EPS, ALU.mult, ALU.add).then_inc(pre.next("pre_dve"), 1)
            dve.wait_ge(pre.sem["std"], 1)
            nc.vector.reciprocal(stat[:, 0, :], stat[:, 1, :]).then_inc(pre.next("pre_dve"), 1)
            dve.wait_ge(pre.sem["pre_dve"], pre.made["pre_dve"])
            for t in range(4):
                nc.vector.tensor_scalar(xrow[:, t, :], xrow[:, t, :], stat[:, 0, t:t + 1], None, ALU.mult).then_inc(pre.next("xn"), 1)
            for n in range(EARLY_MOD):
                dve.wait_ge(env.slab_free, n + 1)
                nc.vector.tensor_copy((bv, ktail)[n // 2][0:2, n % 2].rearrange("p t c -> p (t c)"), ps[(5, 6, 7, 0)[n]][0:2, :]).then_inc(pre.next("mod_row"), 1)
            dve.wait_ge(pre.sem["mod_ps"], 1)
            for c in range(2):
                nc.vector.tensor_tensor(modT[:, c, 0:16], ps[5][:, 0:32].rearrange("p (n c) -> p c n", c=2)[:, c, :], vec[:, 16:32], ALU.add).then_inc(pre.next("pre_dve"), 1)
            dve.wait_ge(pre.sem["pre_dve"], pre.made["pre_dve"])
            for c in range(2):
                nc.vector.scalar_tensor_tensor(coef[:, c, :], modT[:, c, 8:16], 1.0, vec[:, 64:72], ALU.add, ALU.mult).then_inc(pre.next("pre_dve"), 1)
            dve.wait_ge(pre.sem["pre_dve"], pre.made["pre_dve"])
            for k in range(KC):
                dve.wait_ge(pre.sem["uT_ps"], k + 1)
                for c in range(2):
                    o = T if c == 0 else 0
                    nc.vector.tensor_scalar(uT[:, k, o:o + T], ps[1 + k % 4][:, o:o + T], coef[:, c, k:k + 1], modT[:, c, k:k + 1], ALU.mult, ALU.add).then_inc(pre.next("uT_out"), 1)
            dve.wait_ge(pre.sem["ab_ps"], 1)
            nc.vector.tensor_copy(ab[:], ps[6][:, 0:128].rearrange("p (t c) -> p t c", t=4)).then_inc(pre.next("pre_dve"), 1)
            dve.wait_ge(pre.sem["pre_dve"], pre.made["pre_dve"])
            for d in range(2):
                i = nc.vector.tensor_tensor(gt1[:, 0, :, d * 8:d * 8 + 8], ab[:, :, d * 16:d * 16 + 8],
                                            dtb[:, d * 8:d * 8 + 8].unsqueeze(1).to_broadcast((P, 4, 8)), ALU.add)
            i.then_inc(pre.next("ab"), 1)
            dve.wait_ge(pre.sem["softp"], 2)
            nc.vector.scalar_tensor_tensor(gt1[:, 2], gt1[:, 0], 0.0, gt1[:, 1], ALU.max, ALU.add).then_inc(pre.next("pre_dve"), 1)
            dve.wait_ge(pre.sem["pre_dve"], pre.made["pre_dve"])
            nc.vector.scalar_tensor_tensor(gates[:], gt1[:, 2], -1.0, alog[:].unsqueeze(1).to_broadcast((P, 4, 16)), ALU.mult, ALU.mult).then_inc(pre.next("gates"), 1)
            dve.wait_ge(pre.sem["gcum_ps"], 1)
            nc.vector.tensor_copy(scal[:, 0].rearrange("p d t h -> p (d t h)"), ps[7][:, 0:64]).then_inc(pre.next("pre_dve"), 1)
            nc.vector.tensor_copy(scal[:, 4].rearrange("p d t h -> p (d t h)"), ps[7][:, 64:128]).then_inc(pre.next("pre_dve"), 1)
            dve.wait_ge(pre.sem["pre_dve"], pre.made["pre_dve"])
            for d in range(2):
                nc.vector.tensor_scalar(scal[:, 1, d], beta[:, :, d * 8:d * 8 + 8], -1.0, None, ALU.mult)
                nc.vector.tensor_copy(scal[:, 2, d], beta[:, :, d * 8:d * 8 + 8])
            nc.vector.tensor_tensor(scal[:, 3].rearrange("p d t h -> p (d t h)"), ps[7][:, 64:128], scal[:, 0].rearrange("p d t h -> p (d t h)"), ALU.subtract).then_inc(pre.next("gcum"), 1)
            dve.wait_ge(pre.sem["gexp"], 1)
            dve.wait_ge(pre.sem["gcum"], 1)
            dve.wait_ge(pre.sem["first_head"], 3)
            i = nc.vector.tensor_tensor(scal[:, 5], scal[:, 5], scal[:, 1], ALU.mult)
            i.then_inc(hs.sem["head_done"], 1)

            with dve.Fori(0, HEADS) as h:
                dve.wait_ge(hs.sem["head_done"], hs.value(h, "head_done", 1))
                def link(ins):
                    ins.then_inc(hs.next("dself"), 1)
                    dve.wait_ge(hs.sem["dself"], hs.value(h, "dself", hs.made["dself"]))

                link(nc.vector.tensor_copy(hsc[:], scal[:, :, :, :, bass.ds(h, 1)].rearrange("p n d t o -> p n (d t o)")))
                link(nc.vector.tensor_copy(cw[:], vec[:, 96:216].rearrange("p (w j n) -> p j n w", w=5, j=3)[:, :, bass.ds(h, 1), :].rearrange("p j o w -> p j (o w)")))
                for n, (raw, src, s) in enumerate(((kraw, pk[:], 2), (vraw, pv[:], 2), (qraw, pqz[:, 0:T], 1))):
                    dve.wait_ge(hs.sem["tap0"], hs.value(h, "tap0", n + 1))
                    r3 = raw[:, :].rearrange("p (s t) -> p s t", s=s)
                    p3 = src.rearrange("p (s t) -> p s t", s=s)
                    for m, j in enumerate((0, 1, 3, 4)):
                        o = j - 2
                        lo, hi = max(0, -o), T - max(0, o)
                        i = nc.vector.scalar_tensor_tensor(r3[:, :, lo:hi], p3[:, :, lo + o:hi + o], cw[:, (1, 2, 0)[n], j:j + 1], r3[:, :, lo:hi], ALU.mult, ALU.add)
                        if m < 3:
                            link(i)
                        else:
                            i.then_inc(hs.next("conv"), 1)
                dve.wait_ge(hs.sem["row_ps"], hs.value(h, "row_ps", 1))
                for d in range(2):
                    for t in range(4):
                        i = nc.vector.scalar_tensor_tensor(dec[:, d, t, :], ps[6 + d][:, t * P:(t + 1) * P], hsc[:, 0, 4 * d + t:4 * d + t + 1], masks[:, C_BIG + d - N_SHARED, :], ALU.subtract, ALU.add)
                    i.then_inc(hs.next("arg"), 1)
                for d in range(2):
                    for t in range(2, 4):
                        i = nc.vector.scalar_tensor_tensor(decT[:, d, t - 2, :], ps[6 + d][:, t * P:(t + 1) * P], hsc[:, 0, 4 * d + t:4 * d + t + 1], masks[:, C_NEG + d - N_SHARED, :], ALU.subtract, ALU.add)
                    i.then_inc(hs.next("arg"), 1)
                dve.wait_ge(hs.sem["root"], hs.value(h, "root", 1))
                link(nc.vector.reciprocal(rn[:, 0:2 * T], rn[:, 0:2 * T]))
                nc.vector.tensor_tensor(kT[:, :], kraw[:, :], rn[:, 0:2 * T], ALU.mult).then_inc(hs.next("kq_norm"), 1)
                dve.wait_ge(hs.sem["root"], hs.value(h, "root", 2))
                link(nc.vector.reciprocal(rn[:, 2 * T:], rn[:, 2 * T:]))
                nc.vector.scalar_tensor_tensor(qT[:, :], qraw[:, :], float(P) ** -0.5, rn[:, 2 * T:], ALU.mult, ALU.mult).then_inc(hs.next("kq_norm"), 1)
                dve.wait_ge(hs.sem["tok_ps"], hs.value(h, "tok_ps", 1))
                for d in range(2):
                    i = nc.vector.tensor_tensor(bv[:, d], ps[5][:, :].rearrange("p (t c) -> p t c", t=4), hsc[:, 2, 4 * d:4 * d + 4].unsqueeze(2).to_broadcast((P, 4, P)), ALU.mult)
                i.then_inc(hs.next("tok"), 1)
                dve.wait_ge(hs.sem["kk_ps"], hs.value(h, "kk_ps", 1))
                dve.wait_ge(hs.sem["decay"], hs.value(h, "decay", 2))
                for d in range(2):
                    for t in range(4):
                        i = nc.vector.scalar_tensor_tensor(B[:, d, t, :], ps[0][:, t * P:(t + 1) * P], hsc[:, 1, 4 * d + t:4 * d + t + 1], dec[:, d, t, :], ALU.mult, ALU.mult)
                link(i)
                nc.vector.tensor_tensor(B.rearrange("p d t c -> p (d t) c"), B.rearrange("p d t c -> p (d t) c"), ident.unsqueeze(1).to_broadcast((P, 8, P)), ALU.add).then_inc(hs.next("B"), 1)
                dve.wait_ge(hs.sem["tok_ps"], hs.value(h, "tok_ps", 2))
                for d in range(2):
                    nc.vector.tensor_tensor(ktail[:, d], ps[1][:, :].rearrange("p (t c) -> p t c", t=4), hsc[:, 3, 4 * d:4 * d + 4].unsqueeze(2).to_broadcast((P, 4, P)), ALU.mult).then_inc(hs.next("tok"), 1)
                dve.wait_ge(hs.sem["B"], hs.value(h, "B", 1))
                for d in range(2):
                    nc.vector.tensor_tensor(X[:, d], B[:, d], masks[:, C_M1 + d - N_SHARED, :].unsqueeze(1).to_broadcast((P, 4, P)), ALU.mult).then_inc(hs.next("XY1"), 1)
                    dve.wait_ge(hs.sem["BT_ps"], hs.value(h, "BT_ps", d + 1))
                    nc.vector.tensor_tensor(Y[:, d], ps[4 + d][:, :].rearrange("p (t c) -> p t c", t=4), masks[:, C_M1 + 1 - d - N_SHARED, :].unsqueeze(1).to_broadcast((P, 4, P)), ALU.mult).then_inc(hs.next("XY1"), 1)
                dve.wait_ge(hs.sem["qk_ps"], hs.value(h, "qk_ps", 1))
                dve.wait_ge(hs.sem["decay"], hs.value(h, "decay", 5))
                for d in range(2):
                    i = nc.vector.tensor_tensor(att[:, d], ps[2][:, 0:T].rearrange("p (t c) -> p t c", t=2), decT[:, d], ALU.mult)
                i.then_inc(hs.next("att"), 1)
                for d in range(2):
                    i = nc.vector.tensor_tensor(qd[:, d], qT[:].rearrange("p (t c) -> p t c", t=2), erow[:, d], ALU.mult)
                i.then_inc(hs.next("att"), 1)
                for l in range(len(LEVELS)):
                    for d in range(2):
                        dve.wait_ge(hs.sem["G_ps"], hs.value(h, "G_ps", 2 * l + d + 1))
                        if l > 0:
                            dve.wait_ge(hs.sem["XY_ps"], hs.value(h, "XY_ps", 2 * (l - 1) + d + 1))
                        nc.vector.tensor_tensor(GT[:, d], ps[6 + d][:, :].rearrange("p (t c) -> p t c", t=4), masks[:, C_GT + 2 * l + d - N_SHARED, :].unsqueeze(1).to_broadcast((P, 4, P)), ALU.mult).then_inc(hs.next("G"), 1)
                for c in range(4):
                    for d in range(2):
                        t = c if d == 0 else (1, 0, 3, 2)[c]
                        u = 4 * d + t
                        if c == 0:
                            nc.vector.tensor_copy(W[:, d, :], bv[:, d, t, :]).then_inc(hs.next("W"), 1)
                        else:
                            dve.wait_ge(hs.sem["kS_ps"], hs.value(h, "kS_ps", 2 * (c - 1) + d + 1))
                            nc.vector.scalar_tensor_tensor(W[:, d, :], ps[4 + d][:, 0:P], hsc[:, 5, u:u + 1], bv[:, d, t, :], ALU.mult, ALU.add).then_inc(hs.next("W"), 1)
                    if c == 3:
                        continue
                    for d in range(2):
                        t = c if d == 0 else (1, 0, 3, 2)[c]
                        u = 4 * d + t
                        dve.wait_ge(hs.sem["S_ps"], hs.value(h, "S_ps", 2 * c + d + 1))
                        if c == 0:
                            nc.vector.tensor_copy(S[:, d, :], ps[2 + d][:, 0:P]).then_inc(hs.next("S"), 1)
                        else:
                            nc.vector.scalar_tensor_tensor(S[:, d, :], S[:, d, :], hsc[:, 4, u:u + 1], ps[2 + d][:, 0:P], ALU.mult, ALU.add).then_inc(hs.next("S"), 1)
                dve.wait_ge(hs.sem["modT_ps"], hs.value(h, "modT_ps", 1))
                for c in range(2):
                    i = nc.vector.tensor_tensor(modT[:, c, bass.ds(4 * h + 16, 4)], ps[5][:, 0:8].rearrange("p (n c) -> p c n", c=2)[:, c, :],
                                                vec[:, bass.ds(4 * h + 32, 4)], ALU.add)
                i.then_inc(hs.next("modT"), 1)
                dve.wait_ge(hs.sem["o_root"], hs.value(h, "o_root", 1))
                link(nc.vector.reciprocal(rn[:, 0:T], rn[:, 0:T]))
                link(nc.vector.scalar_tensor_tensor(og[:], ps[0][:, 0:T], vec[:, 88:89], rn[:, 0:T], ALU.mult, ALU.mult))
                i = nc.vector.tensor_tensor(oT[:, bass.ds(h, 1), :].rearrange("p o t -> p (o t)"), og[:], zs[:], ALU.mult)
                i.then_inc(hs.next("head_done"), 1)

            for m in range(KC):
                dve.wait_ge(s_h1, m // 2 * 2 + 2)
                i = nc.vector.scalar_tensor_tensor(hT[:, m, :], ps[m // 2][:, (m % 2) * T:(m % 2 + 1) * T], modT[:, 0, 16 + m:17 + m], hT[:, m, :], ALU.mult, ALU.add)
            i.then_inc(env.stage_done, 1)
            dve.wait_ge(env.stage_done, 1)
        hs.close()
        stage.close()
        retire(nc, pre, hs, [s_vec, s_x, s_ab, s_wh, s_wo, s_h1])


GATE_UP_DOWN = (("g", 0), ("u", 0), ("g", 1), ("u", 1), ("d", 0), ("g", 2), ("u", 2), ("d", 1), ("g", 3), ("u", 3),
                ("d", 2), ("d", 3))
EXPERT_SLABS = len(GATE_UP_DOWN)


def slabs_through(kind, j):
    return EARLY_MOD + GATE_UP_DOWN.index((kind, j)) + 1


def expert_slab(env, e, i):
    kind, j = GATE_UP_DOWN[i]
    w = env.inputs[{"g": "moe_w_gate", "u": "moe_w_up", "d": "moe_w_down"}[kind]][0]
    w = w[bass.ds(e, 1)].rearrange("o (k p) n -> p (o k) n", p=P)
    return w[:, j * 4:j * 4 + 4, :] if kind == "d" else w[:, :, j * 512:(j + 1) * 512]


def moe_prefetch(nc, env, sp, first, end):
    for i in range(first, end):
        env.load(sp, i, expert_slab(env, 0, i))


def first_block_moe(nc, env):
    a = env.inputs
    with ExitStack() as ctx:
        def sb(name, shape):
            return ctx.enter_context(nc.sbuf_tensor(name, shape, F32))

        const, ring, ps, hT, modT, vec = env.const, env.ring, env.ps, env.hT, env.modT, env.vec
        ident = const[:, C_ID, :]
        ones = const[:, C_ONES, :]
        S = EXPERTS * CAP
        Q = 4
        uT = sb("moe_uT", [P, KC, T])
        sqm = sb("moe_squares", [P, KC, T])
        rn = sb("moe_rnorm", [P, T])
        coef = sb("moe_coef", [P, KC])
        wr = sb("w_router", [P, KC, EXPERTS])
        aff = sb("affinity", [P, NT, EXPERTS])
        mx = sb("aff_stats", [P, 3, NT])
        utok = sb("u_token_major", [P, NT, D])
        junk = sb("rank_junk", [P, 2, T])
        cnt = sb("rank_counts", [P, 3, NT, EXPERTS])
        pick = sb("one_hot", [P, NT, EXPERTS, CAP])
        gpick = sb("one_hot_gated", [P, NT, EXPERTS, CAP])
        gpT = sb("one_hot_gatedT", [P, 4, T])
        xsT = sb("chosen_xT", [P, KC, S + CAP])
        sg = sb("silu_gate", [P, 2, 512])
        hid = sb("hidden", [P, 2, 512])
        hidT = sb("hiddenT", [P, 4, 4, CAP])
        ys = sb("expert_y", [P, EXPERTS // Q, D])
        xe = sb("expert_xT", [P, KC, CAP])
        s_wr = ctx.enter_context(nc.semaphore("w_router_loaded"))
        pre = Signals(nc, ctx, "moe_pre", {n: 0 for n in (
            "m_sq", "m_sum_ps", "m_root", "m_self", "m_uT", "logit_ps", "m_max", "m_exp", "m_aff", "utok_ps", "utok_out",
            "rank_rows_ps", "ranks", "picked", "gp_ps", "gp_out", "xs_ps", "xs_out", "comb_ps", "m_h2", "f_sq", "f_sum_ps", "f_root")})
        ex = Signals(nc, ctx, "expert", {"silu_gate_done": 4 * Q, "hidden": 4 * Q, "hidT_ps": 4 * Q, "hidT": 4 * Q, "expert_x": Q, "y_out": Q})
        stage = ctx.enter_context(ExitStack())
        block = stage.enter_context(nc.Block())

        @block.sync
        def _(sp):
            sp.dma_start(wr[:], a["moe_w_router"][0].rearrange("(k p) n -> p k n", p=P)).then_inc(s_wr, 16)
            base = EARLY_MOD - NR + 1
            for i in range(NR, EXPERT_SLABS):
                sp.wait_ge(env.slab_free, base + i)
                env.load(sp, i % NR, expert_slab(env, 0, i))
            with sp.Fori(1, EXPERTS) as e:
                for i in range(EXPERT_SLABS):
                    sp.wait_ge(env.slab_free, e * EXPERT_SLABS + base + i)
                    env.load(sp, i % NR, expert_slab(env, e, i))
            env.layer_prefetch(sp)

        @block.tensor
        def _(pe):
            for k in range(KC):
                pe.wait_ge(pre.sem["m_sq"], k + 1)
                i = nc.tensor.matmul(ps[0][:, 0:T], ones, sqm[:, k, :], start=(k == 0), stop=(k == KC - 1))
            i.then_inc(pre.next("m_sum_ps"), 1)
            pe.wait_ge(s_wr, 16)
            pe.wait_ge(pre.sem["m_uT"], KC)
            for t in range(NT):
                for k in range(KC):
                    i = nc.tensor.matmul(ps[1][:, t * EXPERTS:(t + 1) * EXPERTS], uT[:, k, t * P:(t + 1) * P], wr[:, k, :],
                                         start=(t == 0 and k == 0), stop=(k == KC - 1), skip_group_check=True)
            i.then_inc(pre.next("logit_ps"), 1)
            for t in range(NT):
                for k in range(KC):
                    i = nc.tensor.transpose(ps[2 + 2 * t + k // 4][:, (k % 4) * P:(k % 4 + 1) * P], uT[:, k, t * P:(t + 1) * P], ident)
                    if k % 4 == 3:
                        i.then_inc(pre.next("utok_ps"), 1)
            pe.wait_ge(pre.sem["m_aff"], 1)
            for e in range(EXPERTS):
                b = (e // 2) % 8
                if b in (2, 3, 4, 5) and e % 2 == 0:
                    pe.wait_ge(pre.sem["utok_out"], b - 1)
                for t in range(NT):
                    i = nc.tensor.transpose(ps[b][:, (e % 2) * T + t * P:(e % 2) * T + (t + 1) * P], aff[:, t, e:e + 1].to_broadcast((P, P)), ident)
                if e % 2:
                    i.then_inc(pre.next("rank_rows_ps"), 1)
            pe.wait_ge(pre.sem["picked"], 2)
            for k in range(KC):
                if k >= 4:
                    pe.wait_ge(pre.sem["xs_out"], k - 3)
                for t in range(NT):
                    i = nc.tensor.matmul(ps[k % 4][:, :], utok[:, t, k * P:(k + 1) * P], pick[:, t].rearrange("p e s -> p (e s)"), start=(t == 0), stop=(t == NT - 1))
                i.then_inc(pre.next("xs_ps"), 1)
            pe.wait_ge(pre.sem["picked"], 4)
            for g in range(4):
                for t in range(NT):
                    i = nc.tensor.transpose(ps[4 + g // 2][:, (g % 2) * T + t * P:(g % 2) * T + (t + 1) * P],
                                            gpick[:, t, 4 * g:4 * g + 4, :].rearrange("p e s -> p (e s)"), ident)
                if g % 2:
                    i.then_inc(pre.next("gp_ps"), 1)
            pe.wait_ge(pre.sem["xs_out"], KC)
            pe.wait_ge(pre.sem["gp_out"], 2)
            with pe.Fori(0, EXPERTS // Q) as turn:
                for q in range(Q):
                    q0, q1 = q * CAP, (q + 1) * CAP
                    pe.wait_ge(ex.sem["expert_x"], ex.value(turn, "expert_x", q + 1))
                    for i, (kind, j) in enumerate(GATE_UP_DOWN):
                        slot = i % NR
                        if kind == "d":
                            pe.wait_ge(ex.sem["hidden"], ex.value(turn, "hidden", 4 * q + j + 1))
                            for f in range(4):
                                ins = nc.tensor.transpose(ps[4][:, f * P:(f + 1) * P], hid[:, j % 2, f * P:(f + 1) * P], ident)
                            ins.then_inc(ex.next("hidT_ps"), 1)
                            pe.wait_ge(ex.sem["hidT"], ex.value(turn, "hidT", 4 * q + j + 1))
                            if j == 0:
                                pe.wait_ge(ex.sem["y_out"], ex.value(turn, "y_out", q + 1))
                        pe.wait_ge(env.full[slot], turn * (32 * Q) + 16 * (q * 2 + (slot < EARLY_MOD) + i // NR + 1))
                        if kind == "d":
                            for k in range(4):
                                for half in range(2):
                                    ins = nc.tensor.matmul(ps[5 + half][q0:q1, :], hidT[:, j, k, :], ring[:, slot, k * D + half * 512:k * D + (half + 1) * 512],
                                                           start=(j == 0 and k == 0), stop=(j == 3 and k == 3))
                        else:
                            for k in range(KC):
                                ins = nc.tensor.matmul(ps[2 * (j % 2) + (kind == "u")][q0:q1, :], xe[:, k, :], ring[:, slot, k * 512:(k + 1) * 512],
                                                       start=(k == 0), stop=(k == KC - 1))
                        ins.then_inc(env.slab_free, 1)
            pe.wait_ge(ex.sem["y_out"], ex.value(EXPERTS // Q, "y_out", 1))
            for m in range(KC):
                for g in range(4):
                    i = nc.tensor.matmul(ps[m // 2][:, (m % 2) * T:(m % 2 + 1) * T], ys[:, g, m * P:(m + 1) * P], gpT[:, g, :],
                                         start=(m % 2 == 0 and g == 0), stop=(g == 3), skip_group_check=True)
                i.then_inc(pre.next("comb_ps"), 1)
            for k in range(KC):
                pe.wait_ge(pre.sem["f_sq"], k + 1)
                i = nc.tensor.matmul(ps[4][:, 0:T], ones, sqm[:, k, :], start=(k == 0), stop=(k == KC - 1))
            i.then_inc(pre.next("f_sum_ps"), 1)

        @block.scalar
        def _(act):
            for k in range(KC):
                nc.scalar.activation(sqm[:, k, :], hT[:, k, :], ACT.Square).then_inc(pre.next("m_sq"), 1)
            act.wait_ge(pre.sem["m_sum_ps"], 1)
            nc.scalar.activation(rn[:], ps[0][:, 0:T], ACT.Sqrt, bias=env.eps[:, 0:1], scale=1.0 / D).then_inc(pre.next("m_root"), 1)
            act.wait_ge(pre.sem["m_max"], 1)
            for t in range(NT):
                nc.scalar.activation(aff[:, t, :], ps[1][:, t * EXPERTS:(t + 1) * EXPERTS], ACT.Exp, bias=mx[:, 0, t:t + 1],
                                              accum_out=mx[:, 1, t:t + 1]).then_inc(pre.next("m_exp"), 1)
            for n in range(4):
                act.wait_ge(pre.sem["utok_ps"], n + 1)
                nc.scalar.activation(utok[:, n // 2, (n % 2) * 512:(n % 2 + 1) * 512], ps[2 + n][:, :], ACT.Copy).then_inc(pre.next("utok_out"), 1)
            for n in range(2):
                act.wait_ge(pre.sem["gp_ps"], n + 1)
                nc.scalar.activation(gpT[:, 2 * n:2 * n + 2, :].rearrange("p g t -> p (g t)"), ps[4 + n][:, :], ACT.Copy).then_inc(pre.next("gp_out"), 1)
            with act.Fori(0, EXPERTS // Q) as turn:
                def out_of_bank(q, j):
                    act.wait_ge(ex.sem["hidT_ps"], ex.value(turn, "hidT_ps", 4 * q + j + 1))
                    nc.scalar.activation(hidT[:, j], ps[4][:, :].rearrange("p (f s) -> p f s", f=4)[:, :, q * CAP:(q + 1) * CAP], ACT.Copy).then_inc(ex.next("hidT"), 1)

                for q in range(Q):
                    q0, q1 = q * CAP, (q + 1) * CAP
                    for j in range(4):
                        act.wait_ge(env.slab_free, (turn * Q + q) * EXPERT_SLABS + slabs_through("u", j))
                        nc.scalar.activation(sg[q0:q1, j % 2, :], ps[2 * (j % 2)][q0:q1, :], ACT.Silu).then_inc(ex.next("silu_gate_done"), 1)
                        if j >= 1:
                            out_of_bank(q, j - 1)
                    out_of_bank(q, 3)
            for k in range(KC):
                act.wait_ge(pre.sem["m_h2"], k + 1)
                nc.scalar.activation(sqm[:, k, :], hT[:, k, :], ACT.Square).then_inc(pre.next("f_sq"), 1)
            act.wait_ge(pre.sem["f_sum_ps"], 1)
            nc.scalar.activation(rn[:], ps[4][:, 0:T], ACT.Sqrt, bias=env.eps[:, 0:1], scale=1.0 / D).then_inc(pre.next("f_root"), 1)

        @block.vector
        def _(dve):
            def link(ins):
                ins.then_inc(pre.next("m_self"), 1)
                dve.wait_ge(pre.sem["m_self"], pre.made["m_self"])

            link(nc.vector.scalar_tensor_tensor(coef[:], modT[:, 0, 32:40], 1.0, vec[:, 72:80], ALU.add, ALU.mult))
            dve.wait_ge(pre.sem["m_root"], 1)
            link(nc.vector.reciprocal(rn[:], rn[:]))
            for k in range(KC):
                link(nc.vector.scalar_tensor_tensor(uT[:, k, :], hT[:, k, :], coef[:, k:k + 1], rn[:], ALU.mult, ALU.mult))
                nc.vector.tensor_scalar(uT[:, k, :], uT[:, k, :], modT[:, 0, 24 + k:25 + k], None, ALU.add).then_inc(pre.next("m_uT"), 1)
            dve.wait_ge(pre.sem["logit_ps"], 1)
            link(nc.vector.reduce_max(mx[:, 2, :], ps[1][:, 0:NT * EXPERTS].rearrange("p (t e) -> p t e", t=NT), AX_X))
            nc.vector.tensor_scalar(mx[:, 0, :], mx[:, 2, :], -1.0, None, ALU.mult).then_inc(pre.next("m_max"), 1)
            dve.wait_ge(pre.sem["m_exp"], 2)
            link(nc.vector.reciprocal(mx[:, 1, :], mx[:, 1, :]))
            for t in range(NT):
                i = nc.vector.tensor_scalar(aff[:, t, :], aff[:, t, :], mx[:, 1, t:t + 1], None, ALU.mult)
            i.then_inc(pre.next("m_aff"), 1)
            dve.wait_ge(pre.sem["m_aff"], pre.made["m_aff"])
            for e in range(EXPERTS):
                if e % 2 == 0:
                    dve.wait_ge(pre.sem["rank_rows_ps"], e // 2 + 1)
                row = ps[(e // 2) % 8][:, (e % 2) * T:(e % 2 + 1) * T]
                for t in range(NT):
                    if e or t:
                        dve.wait_ge(pre.sem["ranks"], pre.made["ranks"])
                    nc.vector.tensor_scalar(junk[:, 0, :], row, aff[:, t, e:e + 1], 0.0, ALU.is_gt, ALU.add, accum_out=cnt[:, 0, t, e:e + 1]).then_inc(pre.next("ranks"), 1)
                    w = (t + 1) * P
                    nc.vector.scalar_tensor_tensor(junk[:, 1, 0:w], row[:, 0:w], aff[:, t, e:e + 1], const[:, C_TIE + 1 - t:C_TIE + 2, :].rearrange("p a b -> p (a b)"),
                                                            ALU.is_equal, ALU.mult, accum_out=cnt[:, 1, t, e:e + 1]).then_inc(pre.next("ranks"), 1)
            dve.wait_ge(pre.sem["ranks"], pre.made["ranks"])
            link(nc.vector.tensor_tensor(cnt[:, 2], cnt[:, 0], cnt[:, 1], ALU.add))
            for t in range(NT):
                nc.vector.tensor_tensor(pick[:, t], const[:, C_IOTA, 0:CAP].unsqueeze(1).to_broadcast((P, EXPERTS, CAP)),
                                                 cnt[:, 2, t, :].unsqueeze(2).to_broadcast((P, EXPERTS, CAP)), ALU.is_equal).then_inc(pre.next("picked"), 1)
            dve.wait_ge(pre.sem["picked"], 2)
            for t in range(NT):
                nc.vector.tensor_tensor(gpick[:, t], pick[:, t], aff[:, t, :].unsqueeze(2).to_broadcast((P, EXPERTS, CAP)), ALU.mult).then_inc(pre.next("picked"), 1)
            for k in range(KC):
                dve.wait_ge(pre.sem["xs_ps"], k + 1)
                nc.vector.tensor_copy(xsT[:, k, 0:S], ps[k % 4][:, :]).then_inc(pre.next("xs_out"), 1)
            nc.vector.memset(hid[:], 0.0)
            nc.vector.memset(xsT[:, :, S:], 0.0).then_inc(pre.next("xs_out"), 1)
            dve.wait_ge(pre.sem["xs_out"], KC + 1)
            nc.vector.memset(junk[:, 0, 0:1], 0.0).then_inc(ex.sem["y_out"], 1)
            nc.vector.tensor_copy(xe[:], xsT[:, :, 0:CAP]).then_inc(ex.sem["expert_x"], 1)
            with dve.Fori(0, EXPERTS // Q) as turn:
                for q in range(Q):
                    q0, q1 = q * CAP, (q + 1) * CAP
                    for j in range(4):
                        dve.wait_ge(ex.sem["silu_gate_done"], ex.value(turn, "silu_gate_done", 4 * q + j + 1))
                        nc.vector.tensor_tensor(hid[q0:q1, j % 2, :], ps[2 * (j % 2) + 1][q0:q1, :], sg[q0:q1, j % 2, :], ALU.mult).then_inc(ex.next("hidden"), 1)
                    nc.vector.tensor_copy(xe[:], xsT[:, :, bass.ds((turn * Q + q + 1) * CAP, CAP)]).then_inc(ex.next("expert_x"), 1)
                    dve.wait_ge(env.slab_free, (turn * Q + q) * EXPERT_SLABS + slabs_through("d", 3))
                    for half in range(2):
                        ins = nc.vector.tensor_copy(ys[q0:q1, bass.ds(turn, 1), half * 512:(half + 1) * 512].rearrange("p o n -> p (o n)"), ps[5 + half][q0:q1, :])
                    ins.then_inc(ex.next("y_out"), 1)
            for m in range(KC):
                dve.wait_ge(pre.sem["comb_ps"], m // 2 * 2 + 2)
                nc.vector.scalar_tensor_tensor(hT[:, m, :], ps[m // 2][:, (m % 2) * T:(m % 2 + 1) * T], modT[:, 0, 40 + m:41 + m], hT[:, m, :], ALU.mult, ALU.add).then_inc(pre.next("m_h2"), 1)
            dve.wait_ge(pre.sem["f_root"], 1)
            link(nc.vector.reciprocal(rn[:], rn[:]))
            for k in range(KC):
                i = nc.vector.scalar_tensor_tensor(hT[:, k, :], hT[:, k, :], vec[:, 80 + k:81 + k], rn[:], ALU.mult, ALU.mult)
            i.then_inc(env.stage_done, 1)
            dve.wait_ge(env.stage_done, 2)
        ex.close()
        stage.close()
        retire(nc, pre, ex, [s_wr])


def layer_plan():
    up1 = [("w_up1_2", "cols", n * 512, 512) for n in range(2 * FF // 512)]
    up2 = [("w_up2_2", "cols", n * 512, 512) for n in range(2 * FF // 512)]
    down1, down2 = [], []
    for name, out, parts in (("w_down1_2", down1, (3, 3, 3, 3, 3, 3, 2, 2)), ("w_down2_2", down2, (4, 3, 3, 3, 3, 3, 3))):
        k = 0
        for n in parts:
            out.append((name, "rows", k, n))
            k += n
        assert k == FC
    w = [("w_in_2", "cols", 2 * D + n * 512, 512) for n in range(6)]
    w += [("w_in_2", "cols", 5 * D, AH)]
    w += [("w_in_2", "cols", n * 512, 512) for n in range(2)]
    w += [("w_a_2", "blocks", 0, 8), ("w_x_2", "blocks", 0, 8)]
    w += [("w_in_2", "cols", D + n * 512, 512) for n in range(2)]
    w += [("w_in_2", "cols", 5 * D + AH + n * 512, 512) for n in range(4)]
    w += [(name, "cols", n * 512, 512) for name in ("w_lru_out_2", "w_attn_out_2", "w_o_2") for n in range(2)]
    plan = up1 + down1 + w + up2 + down2
    assert len(plan) % NR == 0
    return plan


LAYER_PLAN = layer_plan()
LAYER_SLABS = len(LAYER_PLAN)
SLABS_BEFORE = EARLY_MOD + EXPERTS * EXPERT_SLABS
V_FFN, V_MIX, V_BG, V_CW, V_CB, V_BA, V_BX, V_LAM, V_GQ, V_GK, V_BF, NVL = (0, 96), 8, 16, 32, 64, 72, 80, 88, 104, 105, 106, 107


def layer_slab(env, layer, i):
    name, how, at, n = LAYER_PLAN[i]
    w = env.inputs[name][bass.ds(layer, 1)]
    if how == "blocks":
        return w.rearrange("o n c d -> c (o n) d")
    w = w.rearrange("o (k p) n -> p (o k) n", p=P)
    return w[:, at:at + n, :] if how == "rows" else w[:, :, at:at + n]


def layer_prefetch(nc, env, sp):
    for i in range(NR):
        sp.wait_ge(env.slab_free, SLABS_BEFORE - NR + i + 1)
        env.load(sp, i, layer_slab(env, 0, i))


def second_block(nc, env, out):
    a = env.inputs
    with ExitStack() as ctx:
        def sb(name, shape):
            return ctx.enter_context(nc.sbuf_tensor(name, shape, F32))

        const, ring, ps, hT = env.const, env.ring, env.ps, env.hT
        ident = const[:, C_ID, :]
        ones = const[:, C_ONES, :]
        rows = sb("layer_vec_rows", [P, LAYERS, P])
        vall = sb("layer_vecs_all", [P, LAYERS, NVL])
        vl = sb("layer_vecs", [P, NVL])
        lam = sb("lru_softplus", [P, 5, KC])
        uT = sb("layer_uT", [P, KC, T])
        hid = sb("ffn_hidden", [P, FC, T])
        gates = hid[:, 0:16, :]
        Sx = hid[:, 16:22, :].rearrange("p a b -> p (a b)").rearrange("p (h c) -> p h c", h=4)
        qn = sb("qnT", [P, KC, T])
        kn = sb("knT", [P, KC, T])
        vtok = sb("v_tokens", [P, NT, D])
        xr = sb("lru_x", [P, KC, T])
        sqn = xr
        r = sb("lru_r", [P, KC, T])
        ig = sb("lru_i", [P, KC, T])
        la = xr
        gl = sb("lru_gelu", [P, KC, T])
        oT = uT
        sqb = sb("qk_squares", [P, 512])
        rnb = sb("rnorms", [P, 512])
        pT = sb("probsT", [P, 384])
        fg = sb("forget", [AH, 3, T])
        cumt = sb("cum_tokens", [P, NT, AH])
        mx = sb("attn_stats", [P, 3, NT, 4])
        xrow = r[:].rearrange("p k t -> p (k t)")
        s_rows = ctx.enter_context(nc.semaphore("layer_rows_loaded"))
        s_out = ctx.enter_context(nc.semaphore("out_stored"))
        pre = Signals(nc, ctx, "out", {"rows_zero": 0, "lvecs_ps": 0, "lvecs": 0, "outT_ps": 0, "out_rows": 0})
        ly = Signals(nc, ctx, "layer", {
            "layer_done": 1, "vl": 1, "l_self": 69, "nsq": 12, "nsum_ps": 3, "nroot": 3, "xn": 24,
            "up_ps": 22, "gate_act": 22, "hid": 22, "res": 8,
            "qk_ps": 4, "qk_sq": 8, "qk_sum_ps": 8, "qk_root": 8, "qk_norm": 8, "v_ps": 2, "v_out": 4,
            "f_in": 1, "f_act": 3, "cum": 1, "cumT_ps": 1, "cumt": 1,
            "lx_ps": 2, "xr0": 4, "xr": 4, "ra_ps": 3, "r": 4, "ix_ps": 3, "i": 4, "lg_ps": 2, "lgelu": 4, "g_ps": 4, "gate": 8,
            "lam_y": 1, "lam": 1, "ix": 4, "lexp": 1, "ltanh": 1, "lsqrt": 1, "lru": 4,
            "s_ps": 16, "s_masked": 4, "s_max": 4, "s_exp": 4, "p_norm": 4, "pT_ps": 16, "pT": 16, "o_ps": 4, "o_out": 4,
            "yl_ps": 2, "ml": 4, "ya_ps": 2, "m": 4, "wo_ps": 2})
        stage = ctx.enter_context(ExitStack())
        block = stage.enter_context(nc.Block())

        def full_at(layer, i):
            return layer * (16 * LAYER_SLABS // NR) + 16 * (EXPERTS * EXPERT_SLABS // NR + (i % NR < EARLY_MOD) + i // NR + 1)

        @block.sync
        def _(sp):
            sp.wait_ge(pre.sem["rows_zero"], 1)
            n_rows = 0
            for l in range(LAYERS):
                at = 0
                for name in ("g_ffn1_2", "g_mix_2", "b_gate_2", "conv_w_2", "conv_b_2", "b_a_2", "b_x_2", "lam_2", "g_ffn2_2"):
                    v = a[name][l]
                    v = v.rearrange("w (n p) -> (w n) p", p=P) if len(v.shape) == 2 else v.rearrange("(n p) -> n p", p=P)
                    sp.dma_start(rows[at:at + v.shape[0], l, :], v).then_inc(s_rows, 16)
                    at += v.shape[0]
                    n_rows += 1
                for name in ("g_q_2", "g_k_2"):
                    for half in range(2):
                        sp.dma_start(rows[at:at + 1, l, half * HD:(half + 1) * HD], a[name][l:l + 1, :]).then_inc(s_rows, 16)
                        n_rows += 1
                    at += 1
                sp.dma_start(rows[at:at + 1, l, 0:AH], a["b_forget_2"][l:l + 1, :]).then_inc(s_rows, 16)
                n_rows += 1
                assert at + 1 == NVL
            assert n_rows == 28
            base = SLABS_BEFORE - NR + 1
            for i in range(NR, LAYER_SLABS):
                sp.wait_ge(env.slab_free, base + i)
                env.load(sp, i % NR, layer_slab(env, 0, i))
            with sp.Fori(1, LAYERS) as l:
                for i in range(LAYER_SLABS):
                    sp.wait_ge(env.slab_free, l * LAYER_SLABS + base + i)
                    env.load(sp, i % NR, layer_slab(env, l, i))
            for t in range(NT):
                sp.wait_ge(pre.sem["out_rows"], 2 * t + 2)
                sp.dma_start(out[0, t * P:(t + 1) * P, :], xrow[:, t * D:(t + 1) * D]).then_inc(s_out, 16)
            sp.wait_ge(s_out, 16 * NT)

        @block.gpsimd
        def _(pool):
            nc.gpsimd.memset(rows[:], 0.0).then_inc(pre.next("rows_zero"), 1)

        @block.tensor
        def _(pe):
            pe.wait_ge(s_rows, 16 * 28)
            for l in range(LAYERS):
                i = nc.tensor.transpose(ps[0][:, l * P:l * P + NVL], rows[0:NVL, l, :], const[0:NVL, C_ID, 0:NVL])
            i.then_inc(pre.next("lvecs_ps"), 1)
            with pe.Fori(0, LAYERS) as l:
                pe.wait_ge(ly.sem["layer_done"], ly.value(l, "layer_done", 1))
                slab = [0]

                def take():
                    i = slab[0]
                    pe.wait_ge(env.full[i % NR], full_at(l, i))
                    return ring[:, i % NR, :]

                def used(ins):
                    ins.then_inc(env.slab_free, 1)
                    slab[0] += 1

                def norm(n):
                    for k in range(KC):
                        if k % 2 == 0:
                            pe.wait_ge(ly.sem["nsq"], ly.value(l, "nsq", 4 * n + k // 2 + 1))
                        i = nc.tensor.matmul(ps[0][:, 0:T], ones, sqn[:, k, :], start=(k == 0), stop=(k == KC - 1))
                    i.then_inc(ly.next("nsum_ps"), 1)
                    pe.wait_ge(ly.sem["xn"], ly.value(l, "xn", 8 * n + 8))

                def columns(x, bank_of, name, before):
                    w = take()
                    for b in range(2):
                        before(b)
                        bank = ps[bank_of(b)]
                        for j in (2 * b, 2 * b + 1):
                            for k in range(KC):
                                i = nc.tensor.matmul(bank[:, (j % 2) * T:(j % 2 + 1) * T], w[:, k * 512 + j * P:k * 512 + (j + 1) * P], x[:, k, :],
                                                     start=(j % 2 == 0 and k == 0), stop=(k == KC - 1), skip_group_check=True)
                        if b == 0:
                            i.then_inc(ly.next(name), 1)
                    return i

                def ffn(n):
                    banks = 2 * FC // 2
                    for s in range(banks // 2):
                        def before(b, s=s):
                            at = 2 * s + b - 4
                            if at >= 0:
                                if at < FC // 2:
                                    pe.wait_ge(ly.sem["gate_act"], ly.value(l, "gate_act", 11 * n + at + 1))
                                else:
                                    pe.wait_ge(ly.sem["hid"], ly.value(l, "hid", 11 * n + at - 11 + 1))
                        used(columns(uT, lambda b, s=s: (2 * s + b) % 4, "up_ps", before))
                    k0 = 0
                    while k0 < FC:
                        nk = LAYER_PLAN[slab[0]][3]
                        w = take()
                        pe.wait_ge(ly.sem["hid"], ly.value(l, "hid", 11 * n + (k0 + nk - 1) // 2 + 1))
                        for k in range(k0, k0 + nk):
                            for m in range(KC):
                                i = nc.tensor.matmul(ps[4 + m // 2][:, (m % 2) * T:(m % 2 + 1) * T], w[:, (k - k0) * D + m * P:(k - k0) * D + (m + 1) * P], hid[:, k, :],
                                                     start=(k == 0 and m % 2 == 0), stop=(k == FC - 1), skip_group_check=True)
                        k0 += nk
                        used(i)

                norm(0)
                ffn(0)
                norm(1)

                def qk_sums(b):
                    pe.wait_ge(ly.sem["qk_sq"], ly.value(l, "qk_sq", b + 1))
                    if b >= 2:
                        pe.wait_ge(ly.sem["qk_root"], ly.value(l, "qk_root", b - 1))
                    nc.tensor.matmul(ps[4 + b % 2][:, :], const[:, C_BD, :], sqb[:], start=True, stop=True).then_inc(ly.next("qk_sum_ps"), 1)

                for s in range(4):
                    w = take()
                    for b in (2 * s, 2 * s + 1):
                        if b >= 4:
                            pe.wait_ge(ly.sem["qk_norm"], ly.value(l, "qk_norm", b - 3))
                        for j in range(2):
                            jj = 2 * (b % 2) + j
                            for k in range(KC):
                                i = nc.tensor.matmul(ps[b % 4][:, j * T:(j + 1) * T], w[:, k * 512 + jj * P:k * 512 + (jj + 1) * P], uT[:, k, :],
                                                     start=(j == 0 and k == 0), stop=(k == KC - 1), skip_group_check=True)
                        if b % 2 == 0:
                            i.then_inc(ly.next("qk_ps"), 1)
                        else:
                            used(i)
                        if b >= 1:
                            qk_sums(b - 1)
                for s in range(2):
                    w = take()
                    for t in range(NT):
                        if s == 0 and t == 1:
                            qk_sums(7)
                        pe.wait_ge(ly.sem["qk_norm"], ly.value(l, "qk_norm", 5 + 2 * s + t))
                        for k in range(KC):
                            i = nc.tensor.matmul(ps[2 * s + t][:, :], uT[:, k, t * P:(t + 1) * P], w[:, k * 512:(k + 1) * 512], start=(k == 0), stop=(k == KC - 1))
                        if t == 0:
                            i.then_inc(ly.next("v_ps"), 1)
                    used(i)
                w = take()
                pe.wait_ge(ly.sem["qk_norm"], ly.value(l, "qk_norm", 8))
                for k in range(KC):
                    i = nc.tensor.matmul(ps[4][0:AH, 0:T], w[:, k * AH:(k + 1) * AH], uT[:, k, :], start=(k == 0), stop=(k == KC - 1))
                used(i)

                def lx_before(b, s=0):
                    pe.wait_ge(ly.sem["f_in"], ly.value(l, "f_in", 1)) if s == 1 else None
                used(columns(uT, lambda b: 6 + b, "lx_ps", lambda b: None))
                used(columns(uT, lambda b: 4 + b, "lx_ps", lambda b: lx_before(b, 1)))
                for which in range(2):
                    w = take()
                    for n in range(8):
                        if n % 2 == 0:
                            if which == 0:
                                pe.wait_ge(ly.sem["xr"], ly.value(l, "xr", (n // 2) + 1))
                                pe.wait_ge(ly.sem["v_out"], ly.value(l, "v_out", n // 2 + 1))
                            else:
                                pe.wait_ge(ly.sem["xr"], ly.value(l, "xr", 4))
                        i = nc.tensor.matmul(ps[4 * which + n // 2][:, (n % 2) * T:(n % 2 + 1) * T], w[:, n * P:(n + 1) * P], xr[:, n, :],
                                             start=(n % 2 == 0), stop=True, skip_group_check=True)
                        if n % 2 == 1 and n < 7:
                            i.then_inc(ly.next(("ra_ps", "ix_ps")[which]), 1)
                    used(i)
                for s in range(2):
                    used(columns(uT, lambda b, s=s: 2 * s + b, "lg_ps", lambda b, s=s: pe.wait_ge(ly.sem["r"], ly.value(l, "r", 2 * s + b + 1))))
                for s in range(4):
                    used(columns(uT, lambda b, s=s: (4 + 2 * s + b) % 8, "g_ps",
                                 lambda b, s=s: pe.wait_ge(ly.sem["i"], ly.value(l, "i", 2 * s + b + 1)) if s < 2 else pe.wait_ge(ly.sem["lgelu"], ly.value(l, "lgelu", 2 * (s - 2) + b + 1))))
                pe.wait_ge(ly.sem["cum"], ly.value(l, "cum", 1))
                pe.wait_ge(ly.sem["gate"], ly.value(l, "gate", 8))
                for t in range(NT):
                    i = nc.tensor.matmul(ps[7][:, t * AH:(t + 1) * AH], fg[:, 1, t * P:(t + 1) * P], ident[0:AH, 0:AH], start=(t == 0), stop=True,
                                         skip_group_check=True)
                i.then_inc(ly.next("cumT_ps"), 1)
                for g in range(4):
                    if g >= 1:
                        pe.wait_ge(ly.sem["s_masked"], ly.value(l, "s_masked", g))
                    for hh in range(4):
                        h = 4 * g + hh
                        r0, tile = (h % 2) * HD, h // 2
                        row = ident[0:AH, h:h + 1].to_broadcast((AH, P))
                        for lo, hi, q0 in ((0, P, 0), (P, 384, P)):
                            nc.tensor.matmul(ps[hh][:, lo:hi], qn[r0:r0 + HD, tile, q0:q0 + P], kn[r0:r0 + HD, tile, 0:hi - lo],
                                             start=(lo == 0), stop=False, skip_group_check=True)
                            i = nc.tensor.matmul(ps[hh][:, lo:hi], row, fg[:, 2, 0:hi - lo], start=False, stop=True, skip_group_check=True)
                        i.then_inc(ly.next("s_ps"), 1)
                    pe.wait_ge(ly.sem["p_norm"], ly.value(l, "p_norm", g + 1))
                    if g == 0:
                        pe.wait_ge(ly.sem["cumt"], ly.value(l, "cumt", 1))
                    for hh in range(4):
                        h = 4 * g + hh
                        r0 = (h % 2) * HD
                        n = 4 * g + hh
                        if n >= 2:
                            pe.wait_ge(ly.sem["pT"], ly.value(l, "pT", n - 1))
                        bank = ps[4 + n % 2]
                        nc.tensor.transpose(bank[:, 0:P], Sx[:, hh, 0:P], ident)
                        nc.tensor.transpose(bank[:, P:2 * P], Sx[:, hh, P:2 * P], ident)
                        nc.tensor.transpose(bank[:, 2 * P:3 * P], Sx[:, hh, 2 * P:3 * P], ident).then_inc(ly.next("pT_ps"), 1)
                        pe.wait_ge(ly.sem["pT"], ly.value(l, "pT", n + 1))
                        if hh == 0 and g >= 2:
                            pe.wait_ge(ly.sem["o_out"], ly.value(l, "o_out", g - 1))
                        ob = ps[6 + g % 2][r0:r0 + HD, (hh // 2) * T:(hh // 2 + 1) * T]
                        nc.tensor.matmul(ob, vtok[:, 0, h * HD:(h + 1) * HD], pT[:, 0:T], start=(hh < 2), stop=False, skip_group_check=True)
                        i = nc.tensor.matmul(ob[:, P:], vtok[:, 1, h * HD:(h + 1) * HD], pT[:, T:384], start=False, stop=True, skip_group_check=True)
                    i.then_inc(ly.next("o_ps"), 1)
                for s in range(2):
                    if s == 0:
                        pe.wait_ge(ly.sem["s_masked"], ly.value(l, "s_masked", 4))
                        pe.wait_ge(ly.sem["lru"], ly.value(l, "lru", 4))
                    used(columns(gl, lambda b, s=s: 2 * s + b, "yl_ps", lambda b: None))
                for s in range(2):
                    if s == 0:
                        pe.wait_ge(ly.sem["pT"], ly.value(l, "pT", 16))
                        pe.wait_ge(ly.sem["o_out"], ly.value(l, "o_out", 4))
                    used(columns(oT, lambda b, s=s: 4 + 2 * s + b, "ya_ps", lambda b: None))
                pe.wait_ge(ly.sem["m"], ly.value(l, "m", 4))
                for s in range(2):
                    used(columns(xr, lambda b, s=s: 2 * s + b, "wo_ps", lambda b: None))
                norm(2)
                ffn(1)
                assert slab[0] == LAYER_SLABS
            pe.wait_ge(ly.sem["layer_done"], ly.value(LAYERS, "layer_done", 1))
            for t in range(NT):
                for k in range(KC):
                    i = nc.tensor.transpose(ps[2 * t + k // 4][:, (k % 4) * P:(k % 4 + 1) * P], hT[:, k, t * P:(t + 1) * P], ident)
                    if k % 4 == 3:
                        i.then_inc(pre.next("outT_ps"), 1)

        S_UP = (0, 11 + 8 + 17 + 6)
        S_DOWN_END = (11 + 8 - 1, LAYER_SLABS - 1)
        S_QK, S_V, S_F, S_LX, S_WA, S_WX, S_LG, S_G, S_LO, S_AO, S_WO = 19, 23, 25, 26, 28, 29, 30, 32, 36, 38, 40

        def bank_of_run(l, name, b, first_slab, before=0):
            if b % 2 == 0:
                return ly.sem[name], ly.value(l, name, before + b // 2 + 1)
            return env.slab_free, l * LAYER_SLABS + SLABS_BEFORE + first_slab + b // 2 + 1

        def through(l, i):
            return l * LAYER_SLABS + SLABS_BEFORE + i + 1

        def two(ap):
            return ap.rearrange("p (k t) -> p k t", k=2)

        @block.scalar
        def _(act):
            with act.Fori(0, LAYERS) as l:
                act.wait_ge(ly.sem["layer_done"], ly.value(l, "layer_done", 1))
                act.wait_ge(ly.sem["vl"], ly.value(l, "vl", 1))

                def norm(n):
                    if n > 0:
                        act.wait_ge(ly.sem["res"], ly.value(l, "res", 4 * n))
                    for c in range(4):
                        nc.scalar.activation(sqn[:, 2 * c:2 * c + 2, :], hT[:, 2 * c:2 * c + 2, :], ACT.Square).then_inc(ly.next("nsq"), 1)
                    act.wait_ge(ly.sem["nsum_ps"], ly.value(l, "nsum_ps", n + 1))
                    nc.scalar.activation(rnb[:, 0:T], ps[0][:, 0:T], ACT.Sqrt, bias=env.eps[:, 0:1], scale=1.0 / D).then_inc(ly.next("nroot"), 1)

                def ffn(n):
                    for b in range(FC // 2):
                        act.wait_ge(*bank_of_run(l, "up_ps", b, S_UP[n], 11 * n))
                        nc.scalar.activation(hid[:, 2 * b:2 * b + 2, :], two(ps[b % 4][:, :]), ACT.Silu).then_inc(ly.next("gate_act"), 1)

                act.wait_ge(ly.sem["l_self"], ly.value(l, "l_self", 3))
                nc.scalar.activation(lam[:, 2, :], lam[:, 1, :], ACT.Exp).then_inc(ly.next("lam_y"), 1)
                norm(0)
                ffn(0)
                norm(1)
                for b in range(8):
                    act.wait_ge(*bank_of_run(l, "qk_ps", b, S_QK))
                    if b >= 1:
                        act.wait_ge(ly.sem["qk_sum_ps"], ly.value(l, "qk_sum_ps", b))
                    nc.scalar.activation(sqb[:], ps[b % 4][:, :], ACT.Square).then_inc(ly.next("qk_sq"), 1)
                    if b >= 1:
                        if b >= 2:
                            act.wait_ge(ly.sem["qk_norm"], ly.value(l, "qk_norm", b - 1))
                        nc.scalar.activation(rnb[:], ps[4 + (b - 1) % 2][:, :], ACT.Sqrt, bias=env.eps[:, 0:1], scale=1.0 / HD).then_inc(ly.next("qk_root"), 1)
                act.wait_ge(ly.sem["qk_sum_ps"], ly.value(l, "qk_sum_ps", 8))
                act.wait_ge(ly.sem["qk_norm"], ly.value(l, "qk_norm", 7))
                nc.scalar.activation(rnb[:], ps[5][:, :], ACT.Sqrt, bias=env.eps[:, 0:1], scale=1.0 / HD).then_inc(ly.next("qk_root"), 1)
                for b in range(4):
                    act.wait_ge(*bank_of_run(l, "v_ps", b, S_V))
                    nc.scalar.activation(vtok[:, b % 2, (b // 2) * 512:(b // 2 + 1) * 512], ps[b][:, :], ACT.Copy).then_inc(ly.next("v_out"), 1)
                act.wait_ge(ly.sem["f_in"], ly.value(l, "f_in", 1))
                for n, (f, s, b) in enumerate(((ACT.Abs, 1.0, 0.0), (ACT.Exp, -1.0, 0.0), (ACT.Ln, 1.0, 1.0))):
                    src = fg[:, 0, :] if n == 0 else fg[:, 1, :]
                    nc.scalar.activation(fg[:, 1, :], src, f, scale=s, bias=b).then_inc(ly.next("f_act"), 1)
                    act.wait_ge(ly.sem["f_act"], ly.value(l, "f_act", n + 1))
                for b in range(4):
                    act.wait_ge(*bank_of_run(l, "lx_ps", b, S_LX))
                    for j in range(2):
                        n = 2 * b + j
                        i = nc.scalar.activation(xr[:, n, :], ps[(6, 7, 4, 5)[b]][:, j * T:(j + 1) * T], ACT.Identity,
                                                 scale=vl[:, V_CW + 24 + n:V_CW + 25 + n], bias=vl[:, V_CB + n:V_CB + n + 1])
                    i.then_inc(ly.next("xr0"), 1)
                for which, (dst, bias, name, dn, s) in enumerate(((r, V_BA, "ra_ps", "r", S_WA), (ig, V_BX, "ix_ps", "i", S_WX))):
                    for b in range(4):
                        act.wait_ge(ly.sem[name], ly.value(l, name, b + 1)) if b < 3 else act.wait_ge(env.slab_free, through(l, s))
                        for j in range(2):
                            n = 2 * b + j
                            i = nc.scalar.activation(dst[:, n, :], ps[4 * which + b][:, j * T:(j + 1) * T], ACT.Sigmoid, bias=vl[:, bias + n:bias + n + 1])
                        i.then_inc(ly.next(dn), 1)
                for b in range(4):
                    act.wait_ge(*bank_of_run(l, "lg_ps", b, S_LG))
                    nc.scalar.activation(gl[:, 2 * b:2 * b + 2, :], two(ps[b][:, :]), ACT.Gelu_apprx_tanh).then_inc(ly.next("lgelu"), 1)
                for b in range(8):
                    act.wait_ge(*bank_of_run(l, "g_ps", b, S_G))
                    for j in range(2):
                        n = 2 * b + j
                        i = nc.scalar.activation(gates[:, n, :], ps[(4 + b) % 8][:, j * T:(j + 1) * T], ACT.Sigmoid, bias=vl[:, V_BG + n:V_BG + n + 1])
                    i.then_inc(ly.next("gate"), 1)
                act.wait_ge(ly.sem["lam"], ly.value(l, "lam", 1))
                act.wait_ge(ly.sem["r"], ly.value(l, "r", 4))
                act.wait_ge(ly.sem["ix"], ly.value(l, "ix", 4))
                for n in range(KC):
                    i = nc.scalar.activation(la[:, n, :], r[:, n, :], ACT.Exp, scale=lam[:, 3, n:n + 1])
                i.then_inc(ly.next("lexp"), 1)
                for n in range(KC):
                    i = nc.scalar.activation(r[:, n, :], r[:, n, :], ACT.Tanh, scale=lam[:, 4, n:n + 1])
                i.then_inc(ly.next("ltanh"), 1)
                act.wait_ge(ly.sem["ltanh"], ly.value(l, "ltanh", 1))
                nc.scalar.activation(r[:], r[:], ACT.Sqrt).then_inc(ly.next("lsqrt"), 1)
                for g in range(4):
                    act.wait_ge(ly.sem["s_max"], ly.value(l, "s_max", g + 1))
                    for hh in range(4):
                        for t, (lo, hi) in enumerate(((0, P), (P, 384))):
                            i = nc.scalar.activation(Sx[:, hh, lo:hi], Sx[:, hh, lo:hi], ACT.Exp, bias=mx[:, 1, t, hh:hh + 1], accum_out=mx[:, 2, t, hh:hh + 1])
                    i.then_inc(ly.next("s_exp"), 1)
                    for hh in range(4):
                        act.wait_ge(ly.sem["pT_ps"], ly.value(l, "pT_ps", 4 * g + hh + 1))
                        nc.scalar.activation(pT[:], ps[4 + hh % 2][:, 0:384], ACT.Copy).then_inc(ly.next("pT"), 1)
                    act.wait_ge(ly.sem["o_ps"], ly.value(l, "o_ps", g + 1))
                    nc.scalar.activation(oT[:, 2 * g:2 * g + 2, :], two(ps[6 + g % 2][:, :]), ACT.Copy).then_inc(ly.next("o_out"), 1)
                norm(2)
                ffn(1)

        @block.vector
        def _(dve):
            dve.wait_ge(pre.sem["lvecs_ps"], 1)
            nc.vector.tensor_copy(vall[:], ps[0][:, 0:LAYERS * P].rearrange("p (l n) -> p l n", l=LAYERS)[:, :, 0:NVL]).then_inc(pre.next("lvecs"), 1)
            dve.wait_ge(pre.sem["lvecs"], 1)
            nc.vector.memset(mx[:, 0, 0, 0:1], 0.0).then_inc(ly.sem["layer_done"], 1)
            with dve.Fori(0, LAYERS) as l:
                dve.wait_ge(ly.sem["layer_done"], ly.value(l, "layer_done", 1))

                def link(ins):
                    ins.then_inc(ly.next("l_self"), 1)
                    dve.wait_ge(ly.sem["l_self"], ly.value(l, "l_self", ly.made["l_self"]))

                nc.vector.tensor_copy(vl[:], vall[:, bass.ds(l, 1), :].rearrange("p o n -> p (o n)")).then_inc(ly.next("vl"), 1)
                dve.wait_ge(ly.sem["vl"], ly.value(l, "vl", 1))
                V = vl[:, V_LAM:V_LAM + KC]
                link(nc.vector.tensor_scalar(vl[:, V_GQ:V_GQ + 1], vl[:, V_GQ:V_GQ + 1], HD ** -0.5, None, ALU.mult))
                link(nc.vector.tensor_scalar(lam[:, 0, :], V, -1.0, None, ALU.mult))
                link(nc.vector.tensor_tensor(lam[:, 1, :], V, lam[:, 0, :], ALU.min))
                dve.wait_ge(ly.sem["lam_y"], ly.value(l, "lam_y", 1))
                link(nc.vector.tensor_scalar(lam[:, 1, :], lam[:, 2, :], 2.0, None, ALU.add))
                link(nc.vector.reciprocal(lam[:, 1, :], lam[:, 1, :]))
                link(nc.vector.tensor_tensor(lam[:, 1, :], lam[:, 1, :], lam[:, 2, :], ALU.mult))
                link(nc.vector.tensor_tensor(lam[:, 2, :], lam[:, 1, :], lam[:, 1, :], ALU.mult))
                link(nc.vector.tensor_scalar(lam[:, 3, :], lam[:, 2, :], 2.0 / 17, 2.0 / 15, ALU.mult, ALU.add))
                for odd in (13, 11, 9, 7, 5, 3, 1):
                    link(nc.vector.tensor_tensor(lam[:, 3, :], lam[:, 3, :], lam[:, 2, :], ALU.mult))
                    link(nc.vector.tensor_scalar(lam[:, 3, :], lam[:, 3, :], 2.0 / odd, None, ALU.add))
                link(nc.vector.tensor_tensor(lam[:, 3, :], lam[:, 3, :], lam[:, 1, :], ALU.mult))
                link(nc.vector.scalar_tensor_tensor(lam[:, 2, :], lam[:, 0, :], 0.0, lam[:, 3, :], ALU.max, ALU.add))
                nc.vector.tensor_scalar(lam[:, 3, :], lam[:, 2, :], -LRU_C, None, ALU.mult)
                nc.vector.tensor_scalar(lam[:, 4, :], lam[:, 2, :], LRU_C / 2, None, ALU.mult).then_inc(ly.next("lam"), 1)

                def norm(n):
                    c0 = (V_FFN[0], V_MIX, V_FFN[1])[n]
                    dve.wait_ge(ly.sem["nroot"], ly.value(l, "nroot", n + 1))
                    link(nc.vector.reciprocal(rnb[:, 0:T], rnb[:, 0:T]))
                    for k in range(KC):
                        nc.vector.scalar_tensor_tensor(uT[:, k, :], hT[:, k, :], vl[:, c0 + k:c0 + k + 1], rnb[:, 0:T], ALU.mult, ALU.mult).then_inc(ly.next("xn"), 1)

                def ffn(n):
                    for b in range(FC // 2, FC):
                        dve.wait_ge(*bank_of_run(l, "up_ps", b, S_UP[n], 11 * n))
                        if b == FC // 2:
                            dve.wait_ge(ly.sem["gate_act"], ly.value(l, "gate_act", 11 * n + 11))
                        c = 2 * (b - 11)
                        nc.vector.tensor_tensor(hid[:, c:c + 2, :], two(ps[b % 4][:, :]), hid[:, c:c + 2, :], ALU.mult).then_inc(ly.next("hid"), 1)
                    dve.wait_ge(env.slab_free, through(l, S_DOWN_END[n]))
                    for c in range(4):
                        ins = nc.vector.scalar_tensor_tensor(hT[:, 2 * c:2 * c + 2, :], two(ps[4 + c][:, :]), 0.5, hT[:, 2 * c:2 * c + 2, :], ALU.mult, ALU.add)
                        if n == 0:
                            ins.then_inc(ly.next("res"), 1)
                    return ins

                norm(0)
                ffn(0)
                norm(1)
                for b in range(8):
                    dve.wait_ge(ly.sem["qk_root"], ly.value(l, "qk_root", b + 1))
                    link(nc.vector.reciprocal(rnb[:], rnb[:]))
                    dst, g = (qn, V_GQ) if b < 4 else (kn, V_GK)
                    nc.vector.scalar_tensor_tensor(dst[:, 2 * (b % 4):2 * (b % 4) + 2, :], two(ps[b % 4][:, :]), vl[:, g:g + 1], two(rnb[:]), ALU.mult, ALU.mult).then_inc(ly.next("qk_norm"), 1)
                dve.wait_ge(env.slab_free, through(l, S_F))
                nc.vector.tensor_scalar(fg[:, 0, :], ps[4][0:AH, 0:T], vl[0:AH, V_BF:V_BF + 1], None, ALU.add).then_inc(ly.next("f_in"), 1)
                dve.wait_ge(ly.sem["f_act"], ly.value(l, "f_act", 3))
                link(nc.vector.scalar_tensor_tensor(fg[:, 0, :], fg[:, 0, :], 0.0, fg[:, 1, :], ALU.min, ALU.subtract))
                link(nc.vector.tensor_tensor_scan(fg[:, 1, :], const[0:AH, C_ONES2:C_ONES2 + 2, :].rearrange("p a b -> p (a b)"), fg[:, 0, :], 0.0, ALU.mult, ALU.add))
                nc.vector.tensor_scalar(fg[:, 2, :], fg[:, 1, :], -1.0, None, ALU.mult).then_inc(ly.next("cum"), 1)
                for b in range(4):
                    dve.wait_ge(ly.sem["xr0"], ly.value(l, "xr0", b + 1))
                    for j in range(3):
                        o = 3 - j
                        for m in range(2):
                            n = 2 * b + m
                            i = nc.vector.scalar_tensor_tensor(xr[:, n, o:T], ps[(6, 7, 4, 5)[b]][:, m * T:(m + 1) * T - o], vl[:, V_CW + 8 * j + n:V_CW + 8 * j + n + 1], xr[:, n, o:T], ALU.mult, ALU.add)
                        if j < 2:
                            link(i)
                        else:
                            i.then_inc(ly.next("xr"), 1)
                for c in range(4):
                    dve.wait_ge(ly.sem["i"], ly.value(l, "i", c + 1))
                    if c == 3:
                        dve.wait_ge(env.slab_free, through(l, S_WX))
                    nc.vector.tensor_tensor(ig[:, 2 * c:2 * c + 2, :], ig[:, 2 * c:2 * c + 2, :], xr[:, 2 * c:2 * c + 2, :], ALU.mult).then_inc(ly.next("ix"), 1)
                dve.wait_ge(ly.sem["cumT_ps"], ly.value(l, "cumT_ps", 1))
                nc.vector.tensor_copy(cumt[:], ps[7][:, 0:NT * AH].rearrange("p (t h) -> p t h", t=NT)).then_inc(ly.next("cumt"), 1)
                dve.wait_ge(ly.sem["cumt"], ly.value(l, "cumt", 1))

                def lru(c):
                    if c == 0:
                        dve.wait_ge(ly.sem["lsqrt"], ly.value(l, "lsqrt", 1))
                    sl = slice(2 * c, 2 * c + 2)
                    link(nc.vector.scalar_tensor_tensor(r[:, sl, :], la[:, sl, :], 1.0, r[:, sl, :], ALU.add, ALU.mult))
                    link(nc.vector.tensor_tensor(ig[:, sl, :], ig[:, sl, :], r[:, sl, :], ALU.mult))
                    for n in (2 * c, 2 * c + 1):
                        i = nc.vector.tensor_tensor_scan(r[:, n, :], la[:, n, :], ig[:, n, :], 0.0, ALU.mult, ALU.add)
                    link(i)
                    nc.vector.tensor_tensor(gl[:, sl, :], gl[:, sl, :], r[:, sl, :], ALU.mult).then_inc(ly.next("lru"), 1)

                for g in range(4):
                    for hh in range(4):
                        h = 4 * g + hh
                        dve.wait_ge(ly.sem["s_ps"], ly.value(l, "s_ps", 4 * g + hh + 1))
                        if g >= 1 and hh == 0:
                            dve.wait_ge(ly.sem["pT_ps"], ly.value(l, "pT_ps", 4 * g))
                        nc.vector.scalar_tensor_tensor(Sx[:, hh, 0:P], ps[hh][:, 0:P], cumt[:, 0, h:h + 1], const[:, C_CAUSAL + 1, :], ALU.add, ALU.add)
                        i = nc.vector.scalar_tensor_tensor(Sx[:, hh, P:384], ps[hh][:, P:384], cumt[:, 1, h:h + 1], const[:, C_CAUSAL:C_CAUSAL + 2, :].rearrange("p a b -> p (a b)"), ALU.add, ALU.add)
                    i.then_inc(ly.next("s_masked"), 1)
                    dve.wait_ge(ly.sem["s_masked"], ly.value(l, "s_masked", g + 1))
                    nc.vector.reduce_max(mx[:, 0, 0, :], Sx[:, :, 0:P], AX_X)
                    link(nc.vector.reduce_max(mx[:, 0, 1, :], Sx[:, :, P:384], AX_X))
                    nc.vector.tensor_scalar(mx[:, 1], mx[:, 0], -1.0, None, ALU.mult).then_inc(ly.next("s_max"), 1)
                    lru(g)
                    dve.wait_ge(ly.sem["s_exp"], ly.value(l, "s_exp", g + 1))
                    link(nc.vector.reciprocal(mx[:, 2], mx[:, 2]))
                    nc.vector.tensor_tensor(Sx[:, :, 0:P], Sx[:, :, 0:P], mx[:, 2, 0, :].unsqueeze(2).to_broadcast((P, 4, P)), ALU.mult)
                    nc.vector.tensor_tensor(Sx[:, :, P:384], Sx[:, :, P:384], mx[:, 2, 1, :].unsqueeze(2).to_broadcast((P, 4, 2 * P)), ALU.mult).then_inc(ly.next("p_norm"), 1)
                for b in range(4):
                    dve.wait_ge(*bank_of_run(l, "yl_ps", b, S_LO))
                    nc.vector.tensor_tensor(gates[:, 2 * b:2 * b + 2, :], gates[:, 2 * b:2 * b + 2, :], two(ps[b][:, :]), ALU.mult).then_inc(ly.next("ml"), 1)
                for b in range(4):
                    dve.wait_ge(*bank_of_run(l, "ya_ps", b, S_AO))
                    link(nc.vector.tensor_tensor(gates[:, 8 + 2 * b:10 + 2 * b, :], gates[:, 8 + 2 * b:10 + 2 * b, :], two(ps[4 + b][:, :]), ALU.mult))
                    nc.vector.tensor_tensor(xr[:, 2 * b:2 * b + 2, :], gates[:, 2 * b:2 * b + 2, :], gates[:, 8 + 2 * b:10 + 2 * b, :], ALU.add).then_inc(ly.next("m"), 1)
                for b in range(4):
                    dve.wait_ge(*bank_of_run(l, "wo_ps", b, S_WO))
                    nc.vector.tensor_tensor(hT[:, 2 * b:2 * b + 2, :], two(ps[b][:, :]), hT[:, 2 * b:2 * b + 2, :], ALU.add).then_inc(ly.next("res"), 1)
                norm(2)
                ffn(1).then_inc(ly.next("layer_done"), 1)
            for n in range(4):
                dve.wait_ge(pre.sem["outT_ps"], n + 1)
                nc.vector.tensor_copy(xrow[:, n * 512:(n + 1) * 512], ps[n][:, :]).then_inc(pre.next("out_rows"), 1)
        ly.close()


class Env:
    pass


def build(nc, inputs, out, stages="abc", dbg=None):
    env = Env()
    env.inputs = inputs
    with ExitStack() as ctx:
        env.ctx = ctx
        def sb(name, shape):
            return ctx.enter_context(nc.sbuf_tensor(name, shape, F32))
        env.const = sb("const_masks", [P, N_SHARED, P])
        env.ring = sb("slab_ring", [P, NR, SLAB])
        env.hT = sb("hT", [P, KC, T])
        env.modT = sb("modT", [P, 2, 48])
        env.vec = sb("vec_cols", [P, 216])
        env.eps = sb("eps_col", [P, 1])
        env.ps = [ctx.enter_context(nc.psum_tensor(f"bank{i}", [P, 512], F32)) for i in range(8)]
        env.full = [ctx.enter_context(nc.semaphore(f"slot_full{i}")) for i in range(NR)]
        env.slab_free = env.ctx.enter_context(nc.semaphore("slab_free"))
        env.stage_done = env.ctx.enter_context(nc.semaphore("stage_done"))

        def load(eng, slot, src):
            k, n = src.shape[1], src.shape[2]
            eng.dma_start(env.ring[:, slot, 0:k * n].rearrange("p (k n) -> p k n", k=k), src).then_inc(env.full[slot], 16)
        env.load = load
        if "b" in stages:
            env.moe_prefetch = lambda sp, first, end: moe_prefetch(nc, env, sp, first, end)
        else:
            env.moe_prefetch = lambda sp, first, end: None
        env.layer_prefetch = (lambda sp: layer_prefetch(nc, env, sp)) if "c" in stages else (lambda sp: None)
        first_block_mixer(nc, env)
        if "b" in stages:
            first_block_moe(nc, env)
        if "c" in stages:
            second_block(nc, env, out)
        if dbg is not None:
            s = env.ctx.enter_context(nc.semaphore("dbg"))
            with nc.Block() as block:
                @block.sync
                def _(sp):
                    sp.dma_start(dbg["hT"], env.hT[:]).then_inc(s, 16)
                    sp.wait_ge(s, 16)


def constants():
    import numpy as np
    i = np.arange(P)[:, None]
    j = np.arange(P)[None, :]
    low, up = i > j, i < j
    big = np.float32(3e38) / 4
    out = np.zeros((P, N_CONST, P), np.float32)
    out[:, C_ID] = i == j
    out[:, C_ONES] = 1
    out[:, C_TRIU] = i <= j
    out[:, C_TRIL] = i >= j
    out[:, C_BIG] = np.where(low, 0, big)
    out[:, C_BIG + 1] = np.where(up, 0, big)
    out[:, C_NEG] = np.where(i <= j, 0, -big)
    out[:, C_NEG + 1] = np.where(i >= j, 0, -big)

    out[:, C_ONES:C_TIE + 1] = 1
    out[:, C_BD] = i // HD == j // HD
    out[:, C_CAUSAL + 1] = np.where(i >= j, 0, -big)
    out[:, C_TIE + 1] = low
    out[:, C_IOTA] = j

    def level(s):
        return (i // (2 * s) == j // (2 * s)) & (i // s != j // s)
    out[:, C_M1] = (level(1) & low) | (i == j)
    out[:, C_M1 + 1] = (level(1) & up) | (i == j)
    for n, s in enumerate(LEVELS):
        out[:, C_GT + 2 * n] = (level(s) & up) | (i == j)
        out[:, C_GT + 2 * n + 1] = (level(s) & low) | (i == j)
    return out


_INS = ["x", "c", "ctx", "c_ctx", "w_mod", "b_mod", "norm_mix_g", "norm_ffn_g", "gdn_w_in", "gdn_conv_w", "gdn_a_log",
        "gdn_dt_bias", "gdn_o_gain", "gdn_w_out", "moe_w_router", "moe_w_gate", "moe_w_up", "moe_w_down", "final_g",
        "g_ffn1_2", "w_up1_2", "w_down1_2", "g_mix_2", "w_in_2", "b_gate_2", "conv_w_2", "conv_b_2", "w_a_2", "b_a_2",
        "w_x_2", "b_x_2", "lam_2", "g_q_2", "g_k_2", "b_forget_2", "w_lru_out_2", "w_attn_out_2", "w_o_2", "g_ffn2_2",
        "w_up2_2", "w_down2_2"]


def kernel(**inputs):
    import numpy as _np
    import concourse.bacc as _bacc
    from concourse import mybir as _mybir
    from concourse.bass_utils import run_bass_kernel_spmd as _run

    nc = _bacc.Bacc("TRN2", target_bir_lowering=False, num_devices=1)
    arrays, aps = {}, {}
    for name in _INS:
        arrays[f"in_{name}"] = _np.ascontiguousarray(inputs[name])
        aps[name] = nc.dram_tensor(f"in_{name}", arrays[f"in_{name}"].shape, _mybir.dt.float32, kind="ExternalInput").ap()
    arrays["in_masks"] = constants()
    aps["const"] = nc.dram_tensor("in_masks", arrays["in_masks"].shape, _mybir.dt.float32, kind="ExternalInput").ap()
    out = nc.dram_tensor("out_0", (1, T, D), _mybir.dt.float32, kind="ExternalOutput").ap()
    build(nc, aps, out)
    r = _run(nc, [arrays], core_ids=[0])
    return r.results[0]["out_0"]
```
